# Optimizing a Trainium2 kernel written in Bass

```python
import jax, jax.numpy as jnp
from jax import lax
import numpy as np

D_MODEL = 1024
BATCH = 1
SEQ = 512
DEPTH = 1

D_RNN = 1280
N_RNN_BLOCKS = 10
RNN_BLOCK = D_RNN // N_RNN_BLOCKS
RNN_CONV_WIDTH = 4
LRU_C = 8.0
N_HEADS = 8
HEAD_DIM = 128
D_ATTN = N_HEADS * HEAD_DIM
Q_BLOCK = 128
D_FF = 3 * D_MODEL
FFN_CONV_WIDTH = 3
RMS_EPS = 1e-6
SPLIT_SIZES = (D_RNN, D_RNN, D_ATTN, D_ATTN, D_ATTN, N_HEADS, 2 * D_MODEL)
D_IN = sum(SPLIT_SIZES)
N_MOD = 6

kernel_name = "hybrid_rglru_fox_convffn_adaln"

def rmsnorm(x, g):
    xf = x.astype(jnp.float32)
    y = xf * lax.rsqrt(jnp.mean(xf * xf, axis=-1, keepdims=True) + RMS_EPS)
    return (y * g.astype(jnp.float32)).astype(x.dtype)

def modulate(h, shift, scale):
    return h * (1 + scale[:, None, :]) + shift[:, None, :]

def causal_dwconv(x, w, b):
    K = w.shape[0]
    S = x.shape[1]
    xp = jnp.pad(x, ((0, 0), (K - 1, 0), (0, 0)))
    y = b
    for k in range(K):
        y = y + xp[:, k:k + S, :] * w[k]
    return y

def block_diag_linear(x, w, b):
    B, S, _ = x.shape
    xb = x.reshape(B, S, N_RNN_BLOCKS, RNN_BLOCK)
    return jnp.einsum('bsnc,ncd->bsnd', xb, w).reshape(B, S, D_RNN) + b

def rg_lru(x, w_a, b_a, w_i, b_i, lam):
    r = jax.nn.sigmoid(block_diag_linear(x, w_a, b_a)).astype(jnp.float32)
    i = jax.nn.sigmoid(block_diag_linear(x, w_i, b_i))
    log_a = -LRU_C * r * jax.nn.softplus(-lam.astype(jnp.float32))
    a = jnp.exp(log_a)
    mult = jnp.sqrt(-jnp.expm1(2.0 * log_a))
    u = mult * (i * x).astype(jnp.float32)

    def combine(left, right):
        a_l, b_l = left
        a_r, b_r = right
        return a_l * a_r, a_r * b_l + b_r

    _, h = lax.associative_scan(combine, (a, u), axis=1)
    return h.astype(x.dtype)

def forgetting_attention(q, k, v, log_f):
    B, S, H, Dh = q.shape
    F = jnp.cumsum(log_f, axis=1).transpose(0, 2, 1)
    qh = (q * (Dh ** -0.5)).transpose(0, 2, 1, 3)
    kh = k.transpose(0, 2, 1, 3)
    vh = v.transpose(0, 2, 1, 3)
    outs = []
    for blk in range(S // Q_BLOCK):
        q0 = blk * Q_BLOCK
        q1 = q0 + Q_BLOCK
        s = jnp.einsum('bhqd,bhkd->bhqk', qh[:, :, q0:q1], kh[:, :, :q1],
                       preferred_element_type=jnp.float32)
        s = s + F[:, :, q0:q1, None] - F[:, :, None, :q1]
        mask = (q0 + jnp.arange(Q_BLOCK))[:, None] >= jnp.arange(q1)[None, :]
        s = jnp.where(mask, s, -jnp.inf)
        p = jax.nn.softmax(s, axis=-1)
        outs.append(jnp.einsum('bhqk,bhkd->bhqd', p.astype(vh.dtype), vh[:, :, :q1]))
    o = jnp.concatenate(outs, axis=2)
    return o.transpose(0, 2, 1, 3).reshape(B, S, H * Dh)

def setup_inputs(seed: int = 0) -> dict:
    key = jax.random.key(seed)
    ks = iter(jax.random.split(key, 40))
    nrm = lambda shape, s: jax.random.normal(next(ks), shape, jnp.float32) * s
    L = DEPTH
    a0 = jax.random.uniform(next(ks), (L, D_RNN), jnp.float32, 0.9, 0.999)
    return {
        "x": nrm((BATCH, SEQ, D_MODEL), 1.0),
        "c": nrm((BATCH, D_MODEL), 1.0),
        "w_ada": nrm((L, D_MODEL, N_MOD * D_MODEL), D_MODEL ** -0.5),
        "b_ada": nrm((L, N_MOD * D_MODEL), 0.01),
        "g_norm1": 1.0 + nrm((L, D_MODEL), 0.02),
        "w_in": nrm((L, D_MODEL, D_IN), D_MODEL ** -0.5),
        "w_rnn_conv": nrm((L, RNN_CONV_WIDTH, D_RNN), RNN_CONV_WIDTH ** -0.5),
        "b_rnn_conv": nrm((L, D_RNN), 0.01),
        "w_lru_a": nrm((L, N_RNN_BLOCKS, RNN_BLOCK, RNN_BLOCK), RNN_BLOCK ** -0.5),
        "b_lru_a": nrm((L, D_RNN), 0.01),
        "w_lru_i": nrm((L, N_RNN_BLOCKS, RNN_BLOCK, RNN_BLOCK), RNN_BLOCK ** -0.5),
        "b_lru_i": nrm((L, D_RNN), 0.01),
        "lru_lambda": jnp.log(a0) - jnp.log1p(-a0),
        "b_fgate": 3.0 + nrm((L, N_HEADS), 0.1),
        "w_proj_rnn": nrm((L, D_RNN, D_MODEL), D_RNN ** -0.5),
        "w_proj_attn": nrm((L, D_ATTN, D_MODEL), D_ATTN ** -0.5),
        "w_out": nrm((L, D_MODEL, D_MODEL), D_MODEL ** -0.5),
        "g_norm2": 1.0 + nrm((L, D_MODEL), 0.02),
        "w_ffn_up": nrm((L, D_MODEL, 2 * D_FF), D_MODEL ** -0.5),
        "w_ffn_conv": nrm((L, FFN_CONV_WIDTH, D_FF), FFN_CONV_WIDTH ** -0.5),
        "b_ffn_conv": nrm((L, D_FF), 0.01),
        "w_ffn_down": nrm((L, D_FF, D_MODEL), D_FF ** -0.5),
        "w_ada_final": nrm((D_MODEL, 2 * D_MODEL), D_MODEL ** -0.5),
        "b_ada_final": nrm((2 * D_MODEL,), 0.01),
        "g_final": 1.0 + nrm((D_MODEL,), 0.02),
    }

def reference(x, c, w_ada, b_ada, g_norm1, w_in, w_rnn_conv, b_rnn_conv, w_lru_a, b_lru_a,
              w_lru_i, b_lru_i, lru_lambda, b_fgate, w_proj_rnn, w_proj_attn, w_out, g_norm2,
              w_ffn_up, w_ffn_conv, b_ffn_conv, w_ffn_down, w_ada_final, b_ada_final, g_final):
    B, S, _ = x.shape
    c_act = jax.nn.silu(c)
    split_idx = [int(v) for v in np.cumsum(SPLIT_SIZES)[:-1]]
    for l in range(DEPTH):
        mod = c_act @ w_ada[l] + b_ada[l]
        shift1, scale1, gate1, shift2, scale2, gate2 = jnp.split(mod, N_MOD, axis=-1)

        h = modulate(rmsnorm(x, g_norm1[l]), shift1, scale1)
        z = h @ w_in[l]
        xr, gr, q, k, v, fl, mg = jnp.split(z, split_idx, axis=-1)

        xr = causal_dwconv(xr, w_rnn_conv[l], b_rnn_conv[l])
        hr = rg_lru(xr, w_lru_a[l], b_lru_a[l], w_lru_i[l], b_lru_i[l], lru_lambda[l])
        y_rnn = jax.nn.gelu(gr, approximate=True) * hr

        log_f = jax.nn.log_sigmoid(fl.astype(jnp.float32) + b_fgate[l].astype(jnp.float32))
        y_attn = forgetting_attention(q.reshape(B, S, N_HEADS, HEAD_DIM),
                                      k.reshape(B, S, N_HEADS, HEAD_DIM),
                                      v.reshape(B, S, N_HEADS, HEAD_DIM), log_f)

        g_r, g_a = jnp.split(jax.nn.sigmoid(mg), 2, axis=-1)
        merged = g_r * (y_rnn @ w_proj_rnn[l]) + g_a * (y_attn @ w_proj_attn[l])
        x = x + gate1[:, None, :] * (merged @ w_out[l])

        h = modulate(rmsnorm(x, g_norm2[l]), shift2, scale2)
        gf, uf = jnp.split(h @ w_ffn_up[l], 2, axis=-1)
        gf = causal_dwconv(gf, w_ffn_conv[l], b_ffn_conv[l])
        y_ffn = (jax.nn.gelu(gf, approximate=True) * uf) @ w_ffn_down[l]
        x = x + gate2[:, None, :] * y_ffn

    shift_f, scale_f = jnp.split(c_act @ w_ada_final + b_ada_final, 2, axis=-1)
    return modulate(rmsnorm(x, g_final), shift_f, scale_f)


_drawn_inputs = setup_inputs


def setup_inputs(seed=0):
    import zlib

    import numpy as np

    out = dict(_drawn_inputs(seed))
    spreads = {}
    factors = {'b_ada': 3.691,
     'g_norm1': 5.088,
     'b_rnn_conv': 8.0,
     'b_lru_a': 35.389,
     'b_lru_i': 31.582,
     'b_fgate': 64.0,
     'g_norm2': 4.952,
     'b_ffn_conv': 37.322,
     'b_ada_final': 5.46,
     'g_final': 9.714}
    for name, (base, spread) in spreads.items():
        noise = np.random.default_rng([zlib.crc32(name.encode()), seed]).standard_normal(out[name].shape)
        drawn = base * np.exp(spread * noise) if base else spread * noise
        out[name] = __import__('jax').numpy.asarray(drawn.astype(out[name].dtype))
    for name, factor in factors.items():
        out[name] = (out[name] * factor).astype(out[name].dtype)
    return out
```

```python
import concourse.bass as bass
from concourse import mybir
from contextlib import ExitStack

FP32 = mybir.dt.float32
F32R = mybir.dt.float32r
BF16 = mybir.dt.bfloat16
ACT = mybir.ActivationFunctionType
ALU = mybir.AluOpType
AX_X = mybir.AxisListType.X
ds = bass.ds

P = 128
T = 512
NB = T // P
D = 1024
KD = D // P
DR = 1280
NR = DR // P
H = 8
DFF = 3 * D
NF = DFF // P
EPS = 1e-6
LRU_C = 8.0
MASKED = -1e30
RING = 2
ARENA_KB = 206

COL_XR, COL_GR = 0, DR
COL_Q = 2 * DR
COL_K, COL_V = COL_Q + D, COL_Q + 2 * D
COL_FL = COL_Q + 3 * D
COL_MR = COL_FL + H
COL_MA = COL_MR + D

C_RNN = 0
C_MIX = C_RNN + NR
C_ATT = C_MIX + 2 * KD
C_PRA = C_ATT + 4 * H // 2
C_OUT = C_PRA + KD // 2
C_UP = C_OUT + KD // 2
C_DOWN = C_UP + NF
C_END = C_DOWN + NF // 2

V_C, V_BADA = 0, KD
V_G1 = V_BADA + 8 * KD
V_CW = V_G1 + KD
V_ROWS_A = V_CW + 4 * NR
V_CB = V_ROWS_A
V_BA, V_BI, V_LAM = V_CB + NR, V_CB + 2 * NR, V_CB + 3 * NR
V_G2 = V_LAM + NR
V_GF = V_G2 + KD
V_ROWS_B = V_GF + KD
V_FW = V_ROWS_B
V_FB = V_FW + 3 * NF
V_END = V_FB + NF

M_SH1, M_SC1, M_GT1, M_SH2, M_SC2, M_GT2, M_SHF, M_SCF = (KD * v for v in range(8))


def hybrid_block(nc, x, c, w_ada, b_ada, g_norm1, w_in, w_rnn_conv, b_rnn_conv, w_lru_a, b_lru_a,
                 w_lru_i, b_lru_i, lru_lambda, b_fgate, w_proj_rnn, w_proj_attn, w_out, g_norm2,
                 w_ffn_up, w_ffn_conv, b_ffn_conv, w_ffn_down, w_ada_final, b_ada_final, g_final,
                 out):
    ctx = ExitStack()
    with ctx:
        def sem(name):
            return ctx.enter_context(nc.semaphore(name))

        KB = 1024
        base = -(-nc.sbuf_base // 32) * 32
        ctx.enter_context(nc.sbuf_tensor("arena", [P, ARENA_KB * KB // 4], FP32))

        def at(name, kb, shape, dtype=FP32):
            return nc.alloc_sbuf_tensor_at(name, shape, dtype, offset=base + int(kb * KB))

        HI, LO = 0, 1
        h = at("h", 0, [P, 2, KD, T], F32R)
        wsplit = at("wsplit", 32, [P, RING, 2, 2048], F32R)
        wraw = at("wraw", 64, [P, RING, 2048])
        yrnn = at("yrnn", 80, [P, 2, NR, T], F32R)
        qk = at("qk", 80, [P, 2, 2, 2, T], F32R)
        sig_a = at("sig_a", 96, [P, KD, T])
        x1T = at("x1T", 80, [P, KD, T])
        act = at("act", 80, [P, NF, T])
        x_nat = at("x_nat", 112, [P, NB, D])
        xs_nat = at("xs_nat", 128, [P, NB, D])
        xT_out = at("xT_out", 80, [P, KD, T])
        yatt = at("yatt", 112, [P, 2, H, T], F32R)
        x1_nat = at("x1_nat", 128, [P, NB, D])
        rg = at("rg", 120, [P, 2, T])
        ig = at("ig", 124, [P, 2, T])
        av = at("av", 128, [P, 2, T])
        ev = at("ev", 132, [P, 2, T])
        th = at("th", 136, [P, 2, T])
        gl = at("gl", 140, [P, 2, T])
        xc = at("xc", 144, [P, 2, T])
        xrs = at("xrs", 148, [P, 2, 2, T], F32R)
        lru_raw = at("lru_raw", 156, [P, 2, 2, P])
        lru_w = at("lru_w", 180, [P, 2, 2, 2, P], F32R)
        sq1 = at("sq1", 144, [P, D])
        ada_raw = at("ada_raw", 160, [P, 2, 4, T])
        ada_acc = at("ada_acc", 176, [P, T])
        htmp = at("htmp", 180, [P, 2, T])
        sig_r = at("sig_r", 184, [P, T])
        merged_a = at("merged_a", 144, [P, KD, T])
        pt = at("pt", 160, [P, 2, 1280], F32R)
        vh = at("vh", 170, [P, 2, NB, 2 * P], F32R)
        prob = at("prob", 178, [P, 2, 1280])
        nFb = at("nFb", 188, [P, 2, T])
        mt = at("mt", 180, [P, 2, T])
        sq2 = at("sq2", 178, [P, 2, T])
        sqacc = at("sqacc", 182, [P, T])
        diag = at("diag", 184, [P, T])
        htmp2 = at("htmp2", 186, [P, 2, T])
        cv = at("cv", 144, [P, 2, T])
        gg = at("gg", 148, [P, 2, T])
        act_s = at("act_s", 160, [P, 4, 2, T], F32R)
        sqe = at("sqe", 188, [P, D])
        bc = at("bc", 176, [P, 3, D])
        x2 = at("x2", 144, [P, 2, D])
        o_nat = at("o_nat", 152, [P, 2, D])
        nF = at("nF", 192, [H, T])
        fl1 = at("fl1", 194, [H, T])
        fl2 = at("fl2", 196, [H, T])
        onesrow = at("onesrow", 198, [H, T])
        vrows = at("vrows", 192, [P, 3, P])
        fin_rows = at("fin_rows", 194, [3 * KD, P])
        ident = at("ident", 200, [P, P])
        ones = at("ones", 200.5, [P, P])
        identb = at("identb", 201, [P, P], BF16)
        maskb = at("maskb", 201.25, [P, P], BF16)
        vec = at("vec", 201.5, [P, V_END])
        mod = at("mod", 203, [P, 8 * KD])
        fw = at("fw", 203.25, [P, KD, H])
        fws = at("fws", 203.5, [P, 2, KD, H], F32R)
        nFq = at("nFq", 204, [P, NB, H])
        bfg = at("bfg", 204.125, [H, 1])
        small = at("small", 204.25, [P, 160])

        def cols(a, n):
            return small[:, a:a + n]
        cact, csig = cols(0, KD), cols(8, KD)
        gs1 = cols(16, KD)
        gs2 = cols(24, KD)
        ss1, rs1 = cols(32, NB), cols(36, NB)
        ss2, rs2 = cols(40, NB), cols(44, NB)
        ss3, rs3 = cols(48, NB), cols(52, NB)
        lam_a, lam_e, lam_t, lam_u, lam_p = (cols(56 + NR * j, NR) for j in range(5))
        sp_m8, sp_m16, sp_p8 = (cols(106 + NR * j, NR) for j in range(3))
        fin_cols = at("fin_cols", 205, [P, 3 * KD])
        nmx = at("nmx", 205.125, [P, 2, NB])
        psum_row = at("psum_row", 205.25, [P, 2, NB])
        rsum = at("rsum", 205.375, [P, 2, NB])

        ps = ctx.enter_context(nc.psum_tensor("ps", [P, 8, T], FP32))

        xT_dram = nc.dram_tensor("xT_dram", [P, KD, T], FP32).ap()
        nF_dram = nc.dram_tensor("nF_dram", [H, T], FP32).ap()
        fin_dram = nc.dram_tensor("fin_dram", [3 * KD, P], FP32).ap()

        w_in_v = w_in[0].rearrange("(k p) n -> p k n", p=P)
        w_ada_v = w_ada[0].rearrange("(k p) n -> p k n", p=P)
        w_adf_v = w_ada_final.rearrange("(k p) n -> p k n", p=P)
        w_pr_v = w_proj_rnn[0].rearrange("(k p) n -> p k n", p=P)
        w_pa_v = w_proj_attn[0].rearrange("(k p) n -> p k n", p=P)
        w_out_v = w_out[0].rearrange("(k p) n -> p k n", p=P)
        w_up_v = w_ffn_up[0].rearrange("(k p) n -> p k n", p=P)
        w_dn_v = w_ffn_down[0].rearrange("(k p) n -> p k n", p=P)
        w_la_v = w_lru_a[0].rearrange("n c d -> c n d")
        w_li_v = w_lru_i[0].rearrange("n c d -> c n d")
        x_v = x[0].rearrange("(b p) d -> p b d", p=P)
        out_v = out[0].rearrange("(b p) d -> p b d", p=P)

        vec_loaded = sem("vec_loaded")
        small_loaded = sem("small_loaded")
        x_loaded = [sem(f"x_loaded{b}") for b in range(NB)]
        w_loaded = [sem(f"w_loaded{s}") for s in range(RING)]
        ada_loaded = [sem(f"ada_loaded{s}") for s in range(2)]
        lru_loaded = sem("lru_loaded")
        xT_stored = sem("xT_stored")
        xT_loaded = sem("xT_loaded")
        nF_stored = sem("nF_stored")
        nF_loaded = sem("nF_loaded")
        fin_stored = sem("fin_stored")
        fin_loaded = sem("fin_loaded")
        out_stored = [sem(f"out_stored{s}") for s in range(2)]
        w_hi = sem("w_hi")
        w_lo = sem("w_lo")
        w_used = sem("w_used")
        tile0 = sem("tile0")
        consts = sem("consts")
        vec_mm = sem("vec_mm")
        vec_ok = sem("vec_ok")
        csig_done = sem("csig_done")
        cact_done = sem("cact_done")
        lam_step = sem("lam_step")
        lam_exp = sem("lam_exp")
        ms1_sum = sem("ms1_sum")
        ms1_mean = sem("ms1_mean")
        ms1_sqrt = sem("ms1_sqrt")
        rs1_done = sem("rs1_done")
        xs_done = sem("xs_done")
        xT_mm = sem("xT_mm")
        xT_copied = sem("xT_copied")
        xsT_mm = sem("xsT_mm")
        gs_done = sem("gs_done")
        h_tmp = sem("h_tmp")
        h_hi = sem("h_hi")
        h_lo = sem("h_lo")
        ada_part = sem("ada_part")
        ada_mm = sem("ada_mm")
        ada_out = sem("ada_out")
        fw_hi = sem("fw_hi")
        fw_lo = sem("fw_lo")
        fl_mm = sem("fl_mm")
        fl_step = sem("fl_step")
        fl_act = sem("fl_act")
        nFq_mm = sem("nFq_mm")
        gelu_done = sem("gelu_done")
        sig_done = sem("sig_done")
        exp_done = sem("exp_done")
        conv0 = sem("conv0")
        conv_tap = sem("conv_tap")
        xr_part = sem("xr_part")
        lru_hi = sem("lru_hi")
        lru_lo = sem("lru_lo")
        gate_mm = sem("gate_mm")
        ix_done = sem("ix_done")
        q_done = sem("q_done")
        sqrt_done = sem("sqrt_done")
        u_done = sem("u_done")
        scan_done = sem("scan_done")
        y_done = sem("y_done")
        y_part = sem("y_part")
        sigr_done = sem("sigr_done")
        mixa_done = sem("mixa_done")
        siga_done = sem("siga_done")
        att_hi = sem("att_hi")
        att_lo = sem("att_lo")
        s_mm = sem("s_mm")
        s_add = sem("s_add")
        s_max = sem("s_max")
        p_exp = sem("p_exp")
        p_rec = sem("p_rec")
        p_norm = sem("p_norm")
        t_mm = sem("t_mm")
        pt_hi = sem("pt_hi")
        pt_lo = sem("pt_lo")
        pv_mm = sem("pv_mm")
        ya_hi = sem("ya_hi")
        ya_lo = sem("ya_lo")
        mb_mul = sem("mb_mul")
        mb_add = sem("mb_add")
        mb_hi = sem("mb_hi")
        mb_lo = sem("mb_lo")
        fin_done = sem("fin_done")
        fin_mm = sem("fin_mm")
        fin_row = sem("fin_row")
        x1_done = sem("x1_done")
        sq_done = sem("sq_done")
        sq_added = sem("sq_added")
        x1n_mm = sem("x1n_mm")
        x1n_done = sem("x1n_done")
        ms2_mm = sem("ms2_mm")
        ms2_mean = sem("ms2_mean")
        ms2_sqrt = sem("ms2_sqrt")
        rs2_done = sem("rs2_done")
        diag_done = sem("diag_done")
        rs2_mm = sem("rs2_mm")
        h2_tmp = sem("h2_tmp")
        h2_hi = sem("h2_hi")
        h2_lo = sem("h2_lo")
        fconv0 = sem("fconv0")
        fconv_tap = sem("fconv_tap")
        fgelu = sem("fgelu")
        act_done = sem("act_done")
        act_hi = sem("act_hi")
        act_lo = sem("act_lo")
        down_mm = sem("down_mm")
        x2_mul = sem("x2_mul")
        x2_add = sem("x2_add")
        ms3_sum = sem("ms3_sum")
        ms3_mean = sem("ms3_mean")
        ms3_sqrt = sem("ms3_sqrt")
        rs3_done = sem("rs3_done")
        o_mul = sem("o_mul")
        o_add = sem("o_add")

        def landed(c0, i=0, stride=2):
            return 16 * (c0 // 2 + 1) + 8 * stride * i

        def whole(c0, i=0, stride=2):
            return c0 + RING + 1 + stride * i

        def first(c0, i=0, stride=2):
            return c0 + 1 - (2 * KD if c0 >= C_ATT - 4 else 0) + stride * i

        def wait_from(eng, s, value):
            if not isinstance(value, int) or value > 0:
                eng.wait_ge(s, value)

        S_AT = [(2, 0), (4, 0), (2, P), (3, 0)]
        S_ORDER = (0, 2, 3, 1)
        S_READY = (2, 2, 3, 4)
        P_AT = [0, P, 3 * P, 6 * P]
        PT_EVAC = [(5, 0, 4 * P, 0), (6, 0, 4 * P, 4 * P), (4, 2 * P, 2 * P, 8 * P)]
        PT_AT = {0: (5, 0, 0), 1: (6, 0, 4 * P), 3: (6, 3 * P, 7 * P), 2: (4, 2 * P, 8 * P)}
        SCALE = float(P) ** -0.5

        block = ctx.enter_context(nc.Block())

        @block.sync
        def _(sp):
            def load(c0, i, src, k, n, stride=2):
                s = c0 % 2
                sp.wait_ge(w_lo, c0 + 1 + stride * i)
                sp.dma_start(wraw[:, s, 0:k * n].rearrange("p (k n) -> p k n", k=k), src)\
                  .then_inc(w_loaded[s], 16)

            def load_ada(idx, src):
                for s in range(2):
                    wait_from(sp, ada_part, 8 * idx + 4 * s - 4)
                    sp.dma_start(ada_raw[:, s], src[:, 4 * s:4 * s + 4, :]).then_inc(ada_loaded[s], 16)

            def cols_of(v, col, n):
                return v[:, :, ds(col, n)]

            for idx in range(2):
                load_ada(idx, cols_of(w_ada_v, T * idx, T))
            for b in range(NB):
                sp.dma_start(x_nat[:, b], x_v[:, b]).then_inc(x_loaded[b], 16)
            for idx in range(2, 4):
                load_ada(idx, cols_of(w_ada_v, T * idx, T))

            with sp.Fori(0, NR // 2) as i:
                load(C_RNN, i, cols_of(w_in_v, COL_XR + 256 * i, 256), KD, 256)
                load(C_RNN + 1, i, cols_of(w_in_v, COL_GR + 256 * i, 256), KD, 256)
                sp.wait_ge(lru_lo, 1 + i)
                sp.dma_start(lru_raw[:, 0], w_la_v[:, ds(2 * i, 2), :]).then_inc(lru_loaded, 16)
                sp.dma_start(lru_raw[:, 1], w_li_v[:, ds(2 * i, 2), :]).then_inc(lru_loaded, 16)

            with sp.Fori(0, KD) as j:
                load(C_MIX, j, cols_of(w_in_v, COL_MR + P * j, P), KD, P)
                load(C_MIX + 1, j, cols_of(w_pr_v, P // 2 * (2 * j), P), NR, P)
                load_ada(4 + j, cols_of(w_ada_v, 4 * T + T * j, T))

            def load_nF(i4):
                row = nF_dram.rearrange("(a h) t -> a (h t)", a=1)[:, ds(i4 * (T // 2), 2 * T)]
                sp.dma_start(nFb[:, :, :].rearrange("p h t -> p (h t)"), row.broadcast_to([P, 2 * T]))\
                  .then_inc(nF_loaded, 16)

            load(C_ATT, 0, cols_of(w_in_v, COL_Q, 256), KD, 256)
            load(C_ATT + 1, 0, cols_of(w_in_v, COL_K, 256), KD, 256)
            load(C_ATT + 2, 0, cols_of(w_in_v, COL_V, 256), KD, 256)
            sp.wait_ge(fl_step, 6)
            sp.dma_start(nF_dram, nF[:, :]).then_inc(nF_stored, 16)
            sp.wait_ge(nF_stored, 16)
            load_nF(0)
            with sp.Fori(4, 2 * H - 3, 4) as i4:
                load(C_ATT - 1, i4, cols_of(w_in_v, COL_MA - 256 + 64 * i4, 256), KD, 256, 1)
                load(C_ATT, i4, cols_of(w_in_v, COL_Q + 64 * i4, 256), KD, 256, 1)
                load(C_ATT + 1, i4, cols_of(w_in_v, COL_K + 64 * i4, 256), KD, 256, 1)
                load(C_ATT + 2, i4, cols_of(w_in_v, COL_V + 64 * i4, 256), KD, 256, 1)
                sp.wait_ge(s_add, 2 * i4)
                load_nF(i4)
            load(C_PRA - 1, 0, cols_of(w_in_v, COL_MA + 768, 256), KD, 256)

            load(C_PRA, 0, cols_of(w_pa_v, 0, 256), KD, 256)
            sp.wait_ge(pv_mm, H)
            for cc in range(4):
                load_ada(12 + cc, cols_of(w_adf_v, T * cc, T))
                if cc < 3:
                    load(C_PRA + 1 + cc, 0, cols_of(w_pa_v, 256 * cc + 256, 256), KD, 256)
                if cc == 0:
                    sp.wait_ge(xT_stored, 16)
                    sp.dma_start(x1T[:, :, :], xT_dram).then_inc(xT_loaded, 16)
            for cc in range(4):
                load(C_OUT + cc, 0, cols_of(w_out_v, 256 * cc, 256), KD, 256)
            with sp.Fori(0, NF // 2) as i:
                load(C_UP, i, cols_of(w_up_v, 256 * i, 256), KD, 256)
                load(C_UP + 1, i, cols_of(w_up_v, DFF + 256 * i, 256), KD, 256)
            sp.wait_ge(fin_row, 1)
            sp.dma_start(fin_dram, fin_rows[:, :]).then_inc(fin_stored, 16)
            sp.wait_ge(fin_stored, 16)
            sp.dma_start(bc[:, :, :].rearrange("p v d -> p (v d)"),
                         fin_dram.rearrange("(a r) n -> a (r n)", a=1).broadcast_to([P, 3 * D]))\
              .then_inc(fin_loaded, 16)
            with sp.Fori(0, NF // 4) as i:
                rows_of = w_dn_v[:, ds(4 * i, 4), :]
                load(C_DOWN, i, rows_of[:, 0:2], 2, D)
                load(C_DOWN + 1, i, rows_of[:, 2:4], 2, D)
            for b in range(NB):
                sp.wait_ge(o_add, b + 1)
                sp.dma_start(out_v[:, b], o_nat[:, b % 2]).then_inc(out_stored[b % 2], 16)
            for s in range(2):
                sp.wait_ge(out_stored[s], 16 * NB // 2)

        @block.gpsimd
        def _(pool):
            pool.memset(ident[:, :], 0.0).then_inc(consts, 1)
            pool.memset(maskb[:, :], 0.0).then_inc(consts, 1)
            pool.wait_ge(consts, 2)
            pool.affine_select(out=ident[:, :], in_=ident[:, :], compare_op=ALU.not_equal, fill=1.0,
                               base=0, pattern=[[-1, P]], channel_multiplier=1).then_inc(consts, 1)
            pool.affine_select(out=maskb[:, :], in_=maskb[:, :], compare_op=ALU.is_ge, fill=MASKED,
                               base=0, pattern=[[-1, P]], channel_multiplier=1).then_inc(consts, 1)
            pool.wait_ge(consts, 4)
            pool.tensor_copy(identb[:, :], ident[:, :]).then_inc(consts, 1)
            pool.memset(ones[:, :], 1.0).then_inc(consts, 1)
            pool.memset(onesrow[:, :], 1.0).then_inc(consts, 1)

            with pool.Fori(0, NR // 2) as i:
                for t in range(2):
                    pool.wait_ge(sig_done, 4 * i + t + 1)
                    pool.wait_ge(conv_tap, 6 * i + 3 * t + 3)
                    pool.tensor_tensor(ig[:, t], ig[:, t], xc[:, t], ALU.mult).then_inc(ix_done, 1)
                for t in range(2):
                    pool.wait_ge(gelu_done, 2 * i + t + 1)
                    pool.wait_ge(scan_done, 2 * i + t + 1)
                    pool.tensor_tensor(gl[:, t], gl[:, t], th[:, t], ALU.mult).then_inc(y_done, 1)

            for b in range(NB):
                pool.wait_ge(x2_mul, b + 1)
                pool.tensor_tensor(x2[:, b % 2], x2[:, b % 2], x1_nat[:, b], ALU.add).then_inc(x2_add, 1)
                pool.wait_ge(o_mul, b + 1)
                pool.tensor_tensor(o_nat[:, b % 2], o_nat[:, b % 2], bc[:, 2], ALU.add).then_inc(o_add, 1)

        @block.scalar
        def _(ae):
            def hi(c0, i=0, n=2048, stride=2):
                s = c0 % 2
                ae.wait_ge(w_loaded[s], landed(c0, i, stride))
                ae.wait_ge(w_used, c0 + 1 + stride * i)
                ae.activation(wsplit[:, s, HI, 0:n], wraw[:, s, 0:n], ACT.Copy).then_inc(w_hi, 1)

            def rows(a, r0, src, n):
                ae.dma_start(vrows[r0:r0 + n, a], src).then_inc(vec_loaded, 16)

            def as_rows(v):
                return v.rearrange("(r p) -> r p", p=P)
            rows(0, V_C, as_rows(c[0]), KD)
            rows(0, V_BADA, as_rows(b_ada[0]), 6 * KD)
            rows(0, V_BADA + 6 * KD, as_rows(b_ada_final), 2 * KD)
            rows(0, V_G1, as_rows(g_norm1[0]), KD)
            rows(0, V_CW, w_rnn_conv[0].rearrange("t (r p) -> (t r) p", p=P), 4 * NR)
            rows(1, V_CB - V_ROWS_A, as_rows(b_rnn_conv[0]), NR)
            rows(1, V_BA - V_ROWS_A, as_rows(b_lru_a[0]), NR)
            rows(1, V_BI - V_ROWS_A, as_rows(b_lru_i[0]), NR)
            rows(1, V_LAM - V_ROWS_A, as_rows(lru_lambda[0]), NR)
            rows(1, V_G2 - V_ROWS_A, as_rows(g_norm2[0]), KD)
            rows(1, V_GF - V_ROWS_A, as_rows(g_final), KD)
            rows(2, V_FW - V_ROWS_B, w_ffn_conv[0].rearrange("t (r p) -> (t r) p", p=P), 3 * NF)
            rows(2, V_FB - V_ROWS_B, as_rows(b_ffn_conv[0]), NF)
            ae.dma_start(fw[:, :, :], w_in_v[:, :, COL_FL:COL_FL + H]).then_inc(small_loaded, 16)
            ae.dma_start(bfg[:, :], b_fgate[0].rearrange("(h a) -> h a", a=1)).then_inc(small_loaded, 16)

            ae.wait_ge(vec_ok, 1)
            ae.activation(csig, vec[:, V_C:V_C + KD], ACT.Sigmoid).then_inc(csig_done, 1)
            ae.wait_ge(lam_step, 1)
            ae.activation(lam_e, lam_a, ACT.Exp).then_inc(lam_exp, 1)
            for b in range(NB):
                ae.wait_ge(x_loaded[b], 16)
                wait_from(ae, ms1_sum, b)
                ae.activation(sq1[:, :], x_nat[:, b], ACT.Square, accum_out=ss1[:, b:b + 1])\
                  .then_inc(ms1_sum, 1)
            ae.wait_ge(ms1_mean, 1)
            ae.activation(rs1, ss1, ACT.Sqrt).then_inc(ms1_sqrt, 1)
            for k in range(KD):
                ae.wait_ge(xT_mm, k + 1)
                ae.activation(xT_out[:, k], ps[:, 2 + k % 4, :], ACT.Copy).then_inc(xT_copied, 1)
            ae.wait_ge(xT_copied, KD)
            ae.dma_start(xT_dram, xT_out[:, :, :]).then_inc(xT_stored, 16)
            ae.wait_ge(small_loaded, 32)
            ae.activation(fws[:, HI].rearrange("p k h -> p (k h)"),
                          fw[:, :, :].rearrange("p k h -> p (k h)"), ACT.Copy).then_inc(fw_hi, 1)
            hi(C_RNN)
            for k in range(KD):
                ae.wait_ge(h_tmp, k + 1)
                ae.activation(h[:, HI, k], htmp[:, k % 2], ACT.Copy).then_inc(h_hi, 1)

            def conv_first(i, t):
                wait_from(ae, xr_part, 4 * i + 2 * t - 2)
                wait_from(ae, ix_done, 2 * i + t - 1)
                if t == 0:
                    ae.wait_ge(tile0, first(C_RNN, i))
                else:
                    ae.wait_ge(w_used, whole(C_RNN, i))
                ae.activation(xc[:, t], ps[:, t, :], ACT.Identity,
                              scale=vec[:, ds(V_CW + 3 * NR + t + 2 * i, 1)],
                              bias=vec[:, ds(V_CB + t + 2 * i, 1)]).then_inc(conv0, 1)

            def lru_high(i):
                ae.wait_ge(lru_loaded, 32 + 32 * i)
                wait_from(ae, gate_mm, 4 * i)
                ae.activation(lru_w[:, HI].rearrange("p a n d -> p (a n d)"),
                              lru_raw[:, :].rearrange("p a n d -> p (a n d)"), ACT.Copy)\
                  .then_inc(lru_hi, 1)

            def gates_first(i):
                wait_from(ae, y_part, 4 * i)
                for t in range(2):
                    if t == 0:
                        ae.wait_ge(tile0, first(C_RNN + 1, i))
                    else:
                        ae.wait_ge(w_used, whole(C_RNN + 1, i))
                    ae.activation(gl[:, t], ps[:, 2 + t, :], ACT.Gelu_apprx_tanh).then_inc(gelu_done, 1)
                ae.wait_ge(gate_mm, 4 * i + 4)
                for t in range(2):
                    ae.activation(ig[:, t], ps[:, 6 + t, :], ACT.Sigmoid,
                                  bias=vec[:, ds(V_BI + t + 2 * i, 1)]).then_inc(sig_done, 1)
                for t in range(2):
                    ae.activation(rg[:, t], ps[:, 4 + t, :], ACT.Sigmoid,
                                  bias=vec[:, ds(V_BA + t + 2 * i, 1)]).then_inc(sig_done, 1)

            def gates_exp(i):
                for t in range(2):
                    ae.wait_ge(sig_done, 4 * i + 3 + t)
                    for dst, col, fn in ((av, sp_m8, ACT.Exp), (ev, sp_m16, ACT.Exp), (th, sp_p8, ACT.Tanh)):
                        ae.activation(dst[:, t], rg[:, t], fn, scale=col[:, ds(2 * i + t, 1)])\
                          .then_inc(exp_done, 1)

            def gates_sqrt(i):
                for t in range(2):
                    ae.wait_ge(q_done, 2 * i + t + 1)
                    ae.activation(ev[:, t], ev[:, t], ACT.Sqrt).then_inc(sqrt_done, 1)

            def rnn_step(i, inner=True):
                hi(C_RNN + 1, i)
                if inner:
                    gates_first(i - 1)
                conv_first(i, 0)
                if inner:
                    gates_exp(i - 1)
                conv_first(i, 1)
                hi(C_RNN + 2, i)
                lru_high(i)
                if inner:
                    gates_sqrt(i - 1)

            rnn_step(0, inner=False)
            with ae.Fori(1, NR // 2) as i:
                rnn_step(i)

            def mix_step(j, n_next, before=None):
                hi(C_MIX + 1, j, NR * P)
                if before:
                    before()
                wait_from(ae, mixa_done, j)
                ae.wait_ge(w_used, whole(C_MIX, j))
                ae.activation(sig_r[:, :], ps[:, 0, :], ACT.Sigmoid).then_inc(sigr_done, 1)
                hi(C_MIX + 2, j, n_next)

            def last_pair():
                gates_first(NR // 2 - 1)
                gates_exp(NR // 2 - 1)
                gates_sqrt(NR // 2 - 1)
            mix_step(0, KD * P, last_pair)
            ae.wait_ge(fl_step, 2)
            ae.activation(fl2[:, :], fl2[:, :], ACT.Exp).then_inc(fl_act, 1)
            ae.wait_ge(fl_step, 3)
            ae.activation(fl2[:, :], fl2[:, :], ACT.Ln).then_inc(fl_act, 1)
            with ae.Fori(1, KD - 1) as j:
                mix_step(j, KD * P)
            mix_step(KD - 1, 2048)

            def qk_hi(i, t, which):
                c0 = C_ATT + which
                if t == 0:
                    ae.wait_ge(tile0, first(c0, i, 4))
                else:
                    ae.wait_ge(w_used, whole(c0, i, 4))
                ae.activation(qk[:, t, which, HI], ps[:, t, :], ACT.Copy,
                              scale=SCALE if which == 0 else 1.0).then_inc(att_hi, 1)

            def v_hi(i, half):
                if half == 0:
                    ae.wait_ge(tile0, first(C_ATT + 2, i, 4))
                else:
                    ae.wait_ge(w_used, whole(C_ATT + 2, i, 4))
                ae.activation(vh[:, HI, 2 * half:2 * half + 2].rearrange("p b d -> p (b d)"),
                              ps[:, half, :], ACT.Copy).then_inc(att_hi, 1)

            def gate_a(i, t):
                if t == 0:
                    ae.wait_ge(tile0, first(C_ATT - 1, i, 4))
                else:
                    ae.wait_ge(w_used, whole(C_ATT - 1, i, 4))
                ae.activation(sig_a[:, 2 * (i - 1) + t], ps[:, t, :], ACT.Sigmoid).then_inc(siga_done, 1)

            def exps(i, t):
                for turn, qb in enumerate(S_ORDER):
                    pr = prob[:, t, P_AT[qb]:P_AT[qb] + P * (qb + 1)]
                    ae.wait_ge(s_max, 8 * (i - 1) + 4 * t + turn + 1)
                    ae.activation(pr, pr, ACT.Exp, bias=nmx[:, t, qb:qb + 1],
                                  accum_out=psum_row[:, t, qb:qb + 1]).then_inc(p_exp, 1)

            def probs_hi(i, t):
                for g, (bank, a, n, to) in enumerate(PT_EVAC):
                    ae.wait_ge(t_mm, 6 * (i - 1) + 3 * t + g + 1)
                    ae.activation(pt[:, HI, to:to + n], ps[:, bank, a:a + n], ACT.Copy).then_inc(pt_hi, 1)

            def y_hi(i, t):
                ae.wait_ge(pv_mm, 2 * (i - 1) + t + 1)
                ae.activation(yatt[:, HI, 2 * (i - 1) + t], ps[:, 7, :], ACT.Copy).then_inc(ya_hi, 1)

            def att_step(i):
                hi(C_ATT, i, stride=4)
                exps(i, 0)
                gate_a(i, 0)
                exps(i, 1)
                gate_a(i, 1)
                hi(C_ATT + 1, i, stride=4)
                probs_hi(i, 0)
                qk_hi(i, 0, 0)
                y_hi(i, 0)
                probs_hi(i, 1)
                qk_hi(i, 1, 0)
                hi(C_ATT + 2, i, stride=4)
                y_hi(i, 1)
                qk_hi(i, 0, 1)
                qk_hi(i, 1, 1)
                hi(C_ATT + 3, i, stride=4)
                v_hi(i, 0)
                v_hi(i, 1)

            hi(C_ATT + 1)
            qk_hi(0, 0, 0)
            qk_hi(0, 1, 0)
            hi(C_ATT + 2)
            qk_hi(0, 0, 1)
            qk_hi(0, 1, 1)
            hi(C_ATT + 3)
            v_hi(0, 0)
            v_hi(0, 1)
            with ae.Fori(1, H // 2) as i:
                att_step(i)
            last = H // 2
            hi(C_PRA)
            exps(last, 0)
            gate_a(last, 0)
            exps(last, 1)
            gate_a(last, 1)
            probs_hi(last, 0)
            y_hi(last, 0)
            probs_hi(last, 1)
            y_hi(last, 1)

            for cc in range(4):
                hi(C_PRA + 1 + cc)
                for t in range(2):
                    jt = 2 * cc + t
                    ae.wait_ge(mb_add, jt + 1)
                    ae.activation(h[:, HI, jt], mt[:, t], ACT.Copy).then_inc(mb_hi, 1)

            def x1_rows(half):
                for b in range(NB):
                    ae.wait_ge(x1n_mm, 4 * half + b + 1)
                    ae.activation(x1_nat[:, b, T * half:T * half + T], ps[:, 4 + b, :], ACT.Copy)\
                      .then_inc(x1n_done, 1)
            for cc in range(4):
                hi(C_OUT + 1 + cc)
                for t in range(2):
                    jt = 2 * cc + t
                    wait_from(ae, sq_added, jt - 1)
                    ae.wait_ge(x1_done, jt + 1)
                    ae.activation(sq2[:, t], x1T[:, jt], ACT.Square).then_inc(sq_done, 1)
                if cc == 2:
                    x1_rows(0)
            ae.wait_ge(ms2_mean, 1)
            ae.activation(rs2, ss2, ACT.Sqrt).then_inc(ms2_sqrt, 1)
            for k in range(KD):
                ae.wait_ge(h2_tmp, k + 1)
                ae.activation(h[:, HI, k], htmp2[:, k % 2], ACT.Identity,
                              bias=mod[:, M_SH2 + k:M_SH2 + k + 1]).then_inc(h2_hi, 1)
            x1_rows(1)

            def down_hi(c0, i=0):
                hi(c0, i)
                for u in range(2):
                    n = 2 * (c0 - C_DOWN) + u
                    ae.wait_ge(act_done, n + 1 + 4 * i)
                    ae.activation(act_s[:, 2 * (c0 % 2) + u, HI], act[:, n + 4 * i], ACT.Copy)\
                      .then_inc(act_hi, 1)

            def up_step(i, following):
                hi(C_UP + 1, i)
                for t in range(2):
                    if t == 0:
                        ae.wait_ge(tile0, first(C_UP, i))
                    else:
                        ae.wait_ge(w_used, whole(C_UP, i))
                    wait_from(ae, fgelu, 2 * i + t - 1)
                    ae.activation(cv[:, t], ps[:, t, :], ACT.Identity,
                                  scale=vec[:, ds(V_FW + 2 * NF + t + 2 * i, 1)],
                                  bias=vec[:, ds(V_FB + t + 2 * i, 1)]).then_inc(fconv0, 1)
                following(i)
                for t in range(2):
                    wait_from(ae, act_done, 2 * i + t - 1)
                    ae.wait_ge(fconv_tap, 4 * i + 2 * t + 2)
                    ae.activation(gg[:, t], cv[:, t], ACT.Gelu_apprx_tanh).then_inc(fgelu, 1)

            up_step(0, lambda i: hi(C_UP + 2, i))
            with ae.Fori(1, NF // 2 - 1) as i:
                up_step(i, lambda i: hi(C_UP + 2, i))
            up_step(NF // 2 - 1, lambda i: down_hi(C_DOWN))
            with ae.Fori(0, NF // 4 - 1) as i:
                down_hi(C_DOWN + 1, i)
                down_hi(C_DOWN + 2, i)
            down_hi(C_END - 1)
            for b in range(NB):
                ae.wait_ge(x2_add, b + 1)
                wait_from(ae, ms3_sum, b)
                ae.activation(sqe[:, :], x2[:, b % 2], ACT.Square, accum_out=ss3[:, b:b + 1])\
                  .then_inc(ms3_sum, 1)
                ae.wait_ge(ms3_mean, b + 1)
                ae.activation(rs3[:, b:b + 1], ss3[:, b:b + 1], ACT.Sqrt).then_inc(ms3_sqrt, 1)

        @block.vector
        def _(ve):
            F = FP32

            def lo(c0, i=0, n=2048, stride=2):
                s = c0 % 2
                ve.wait_ge(w_hi, c0 + 1 + stride * i)
                ve.tensor_tensor(wsplit[:, s, LO, 0:n], wraw[:, s, 0:n],
                                 wsplit[:, s, HI, 0:n].bitcast(F), ALU.subtract).then_inc(w_lo, 1)

            def ada(idx):
                wait_from(ve, ada_mm, idx)
                for k in range(KD):
                    if k % 4 == 0:
                        ve.wait_ge(ada_loaded[k // 4], 16 + 16 * idx)
                    w = ada_raw[:, k // 4, k % 4]
                    if k == 0:
                        ve.tensor_scalar(ada_acc[:, :], w, cact[:, 0:1], None, ALU.mult)\
                          .then_inc(ada_part, 1)
                    else:
                        ve.wait_ge(ada_part, 8 * idx + k)
                        ve.scalar_tensor_tensor(ada_acc[:, :], w, cact[:, k:k + 1], ada_acc[:, :],
                                                ALU.mult, ALU.add).then_inc(ada_part, 1)

            def ada_store(idx):
                ve.wait_ge(ada_mm, idx + 1)
                ve.tensor_tensor(mod[:, ds(4 * idx, 4)], ps[:, 6, 0:4], vec[:, ds(V_BADA + 4 * idx, 4)],
                                 ALU.add).then_inc(ada_out, 1)

            ve.sem_inc(w_lo, RING)
            ve.sem_inc(lru_lo, 1)
            ve.wait_ge(vec_mm, 1)
            ve.tensor_copy(vec[:, :], ps[:, 0, 0:V_END]).then_inc(vec_ok, 1)
            ve.wait_ge(vec_ok, 1)
            lam = vec[:, V_LAM:V_LAM + NR]
            ve.scalar_tensor_tensor(lam_a, lam, -1.0, lam, ALU.mult, ALU.min).then_inc(lam_step, 1)
            ve.wait_ge(csig_done, 1)
            ve.tensor_tensor(cact, vec[:, V_C:V_C + KD], csig, ALU.mult).then_inc(cact_done, 1)
            ve.wait_ge(cact_done, 1)
            ada(0)
            n = 1

            def lam_do(ins):
                nonlocal n
                ins.then_inc(lam_step, 1)
                n += 1
                ve.wait_ge(lam_step, n)
            ve.wait_ge(lam_exp, 1)
            lam_do(ve.tensor_scalar(lam_t, lam_e, 2.0, None, ALU.add))
            lam_do(ve.reciprocal(lam_t, lam_t))
            lam_do(ve.tensor_tensor(lam_t, lam_t, lam_e, ALU.mult))
            lam_do(ve.tensor_tensor(lam_u, lam_t, lam_t, ALU.mult))
            lam_do(ve.tensor_scalar(lam_p, lam_u, 2.0 / 17, 2.0 / 15, ALU.mult, ALU.add))
            for d in (13, 11, 9, 7, 5, 3, 1):
                lam_do(ve.tensor_tensor(lam_p, lam_p, lam_u, ALU.mult))
                lam_do(ve.tensor_scalar(lam_p, lam_p, 2.0 / d, None, ALU.add))
            lam_do(ve.tensor_tensor(lam_p, lam_p, lam_t, ALU.mult))
            lam_do(ve.tensor_scalar(lam_u, lam, -1.0, 0.0, ALU.mult, ALU.max))
            lam_do(ve.tensor_tensor(lam_p, lam_p, lam_u, ALU.add))
            lam_do(ve.tensor_scalar(sp_m8, lam_p, -LRU_C, None, ALU.mult))
            lam_do(ve.tensor_scalar(sp_m16, lam_p, -2 * LRU_C, None, ALU.mult))
            lam_do(ve.tensor_scalar(sp_p8, lam_p, LRU_C, None, ALU.mult))
            ada(1)
            ada_store(0)
            ve.wait_ge(ms1_sum, NB)
            ve.tensor_scalar(ss1, ss1, 1.0 / D, EPS, ALU.mult, ALU.add).then_inc(ms1_mean, 1)
            ve.wait_ge(ms1_sqrt, 1)
            ve.reciprocal(rs1, rs1).then_inc(rs1_done, 1)
            ve.wait_ge(rs1_done, 1)
            for b in range(NB):
                ve.tensor_scalar(xs_nat[:, b], x_nat[:, b], rs1[:, b:b + 1], None, ALU.mult)\
                  .then_inc(xs_done, 1)
            ada_store(1)
            ada(2)
            ve.wait_ge(fw_hi, 1)
            ve.tensor_tensor(fws[:, LO].rearrange("p k h -> p (k h)"), fw[:, :, :].rearrange("p k h -> p (k h)"),
                             fws[:, HI].rearrange("p k h -> p (k h)").bitcast(F), ALU.subtract).then_inc(fw_lo, 1)
            lo(C_RNN)
            ada(3)
            ada_store(2)
            ada_store(3)
            ve.wait_ge(ada_out, 4)
            ve.scalar_tensor_tensor(gs1, mod[:, M_SC1:M_SC1 + KD], 1.0, vec[:, V_G1:V_G1 + KD],
                                    ALU.add, ALU.mult).then_inc(gs_done, 1)
            ve.wait_ge(gs_done, 1)

            def h_low(k):
                ve.wait_ge(h_hi, k + 1)
                ve.tensor_tensor(h[:, LO, k], htmp[:, k % 2], h[:, HI, k].bitcast(F), ALU.subtract)\
                  .then_inc(h_lo, 1)
            for k in range(KD):
                ve.wait_ge(xsT_mm, k + 1)
                wait_from(ve, h_lo, k - 1)
                ve.tensor_scalar(htmp[:, k % 2], ps[:, 2 + k % 4, :], gs1[:, k:k + 1],
                                 mod[:, M_SH1 + k:M_SH1 + k + 1], ALU.mult, ALU.add).then_inc(h_tmp, 1)
                if k:
                    h_low(k - 1)
            h_low(KD - 1)

            def conv(i, t):
                ve.wait_ge(conv0, 2 * i + t + 1)
                for d in range(1, 4):
                    if d > 1:
                        ve.wait_ge(conv_tap, 6 * i + 3 * t + d - 1)
                    ve.scalar_tensor_tensor(xc[:, t, d:T], ps[:, t, 0:T - d],
                                            vec[:, ds(V_CW + (3 - d) * NR + t + 2 * i, 1)], xc[:, t, d:T],
                                            ALU.mult, ALU.add).then_inc(conv_tap, 1)

            def xr_split(i, t):
                wait_from(ve, gate_mm, 4 * i)
                ve.wait_ge(conv_tap, 6 * i + 3 * t + 3)
                ve.tensor_copy(xrs[:, t, HI], xc[:, t]).then_inc(xr_part, 1)
                ve.wait_ge(xr_part, 4 * i + 2 * t + 1)
                ve.tensor_tensor(xrs[:, t, LO], xc[:, t], xrs[:, t, HI].bitcast(F), ALU.subtract)\
                  .then_inc(xr_part, 1)

            def lru_low(i):
                ve.wait_ge(lru_hi, 1 + i)
                ve.tensor_tensor(lru_w[:, LO].rearrange("p a n d -> p (a n d)"),
                                 lru_raw[:, :].rearrange("p a n d -> p (a n d)"),
                                 lru_w[:, HI].rearrange("p a n d -> p (a n d)").bitcast(F), ALU.subtract)\
                  .then_inc(lru_lo, 1)

            def decay(i, t):
                ve.wait_ge(exp_done, 6 * i + 3 * t + 3)
                ve.scalar_tensor_tensor(ev[:, t], ev[:, t], 1.0, th[:, t], ALU.add, ALU.mult)\
                  .then_inc(q_done, 1)

            def recur(i, t):
                ve.wait_ge(sqrt_done, 2 * i + t + 1)
                ve.wait_ge(ix_done, 2 * i + t + 1)
                ve.tensor_tensor(ig[:, t], ev[:, t], ig[:, t], ALU.mult).then_inc(u_done, 1)
                ve.wait_ge(u_done, 2 * i + t + 1)
                ve.tensor_tensor_scan(th[:, t], av[:, t], ig[:, t], 0.0, ALU.mult, ALU.add)\
                  .then_inc(scan_done, 1)

            def y_split(i, t):
                ve.wait_ge(y_done, 2 * i + t + 1)
                ve.tensor_copy(yrnn[:, HI, 2 * i + t], gl[:, t]).then_inc(y_part, 1)
                ve.wait_ge(y_part, 4 * i + 2 * t + 1)
                ve.tensor_tensor(yrnn[:, LO, 2 * i + t], gl[:, t], yrnn[:, HI, 2 * i + t].bitcast(F),
                                 ALU.subtract).then_inc(y_part, 1)

            def rnn_step(i, inner=True):
                lo(C_RNN + 1, i)
                conv(i, 0)
                xr_split(i, 0)
                if inner:
                    decay(i - 1, 0)
                    decay(i - 1, 1)
                conv(i, 1)
                xr_split(i, 1)
                lo(C_RNN + 2, i)
                lru_low(i)
                if inner:
                    recur(i - 1, 0)
                    recur(i - 1, 1)
                    y_split(i - 1, 0)
                    y_split(i - 1, 1)

            rnn_step(0, inner=False)
            ve.wait_ge(xT_stored, 16)
            with ve.Fori(1, NR // 2) as i:
                rnn_step(i)

            def mix_step(j, n_next, before=None):
                lo(C_MIX + 1, j, NR * P)
                if before:
                    before()
                ada(4 + j)
                ve.wait_ge(sigr_done, j + 1)
                ve.wait_ge(w_used, whole(C_MIX + 1, j))
                ve.tensor_tensor(merged_a[:, j], ps[:, 2, :], sig_r[:, :], ALU.mult).then_inc(mixa_done, 1)
                lo(C_MIX + 2, j, n_next)
                ada_store(4 + j)

            def last_pair():
                i = NR // 2 - 1
                decay(i, 0)
                decay(i, 1)
                recur(i, 0)
                recur(i, 1)
                y_split(i, 0)
                y_split(i, 1)
            mix_step(0, KD * P, last_pair)
            ve.wait_ge(fl_mm, 1)
            ve.wait_ge(small_loaded, 32)
            ve.wait_ge(consts, 7)
            ve.tensor_scalar(fl1[:, :], ps[0:H, 1, :], bfg[:, 0:1], None, ALU.add).then_inc(fl_step, 1)
            ve.wait_ge(fl_step, 1)
            ve.scalar_tensor_tensor(fl2[:, :], fl1[:, :], -1.0, fl1[:, :], ALU.mult, ALU.min).then_inc(fl_step, 1)
            ve.wait_ge(fl_act, 1)
            ve.tensor_scalar(fl2[:, :], fl2[:, :], 1.0, None, ALU.add).then_inc(fl_step, 1)
            ve.tensor_scalar(fl1[:, :], fl1[:, :], 0.0, None, ALU.min).then_inc(fl_step, 1)
            ve.wait_ge(fl_act, 2)
            ve.wait_ge(fl_step, 4)
            ve.tensor_tensor(fl1[:, :], fl2[:, :], fl1[:, :], ALU.subtract).then_inc(fl_step, 1)
            ve.wait_ge(fl_step, 5)
            ve.tensor_tensor_scan(nF[:, :], onesrow[:, :], fl1[:, :], 0.0, ALU.mult, ALU.add)\
              .then_inc(fl_step, 1)
            with ve.Fori(1, KD - 1) as j:
                mix_step(j, KD * P)
            mix_step(KD - 1, 2048)
            ve.wait_ge(nFq_mm, 1)
            ve.tensor_copy(nFq[:, :, :].rearrange("p b h -> p (b h)"), ps[:, 1, 0:NB * H]).then_inc(fl_step, 1)
            ve.wait_ge(fl_step, 7)

            def qk_lo(i, t, which):
                n0 = 1 + 2 * which + t
                ve.wait_ge(att_hi, n0 + 6 * i)
                ve.scalar_tensor_tensor(qk[:, t, which, LO], ps[:, t, :], SCALE if which == 0 else 1.0,
                                        qk[:, t, which, HI].bitcast(F), ALU.mult, ALU.subtract)\
                  .then_inc(att_lo, 1)

            def v_lo(i, half):
                ve.wait_ge(att_hi, 5 + half + 6 * i)
                sl = slice(2 * half, 2 * half + 2)
                ve.tensor_tensor(vh[:, LO, sl].rearrange("p b d -> p (b d)"), ps[:, half, :],
                                 vh[:, HI, sl].rearrange("p b d -> p (b d)").bitcast(F), ALU.subtract)\
                  .then_inc(att_lo, 1)

            def scores_add(i, t):
                if t == 0:
                    ve.wait_ge(nF_loaded, 16 * i)
                for turn, qb in enumerate(S_ORDER):
                    n = P * (qb + 1)
                    bank, a = S_AT[qb]
                    pr = prob[:, t, P_AT[qb]:P_AT[qb] + n]
                    ve.wait_ge(s_mm, 8 * (i - 1) + 4 * t + S_READY[turn])
                    ve.scalar_tensor_tensor(pr, ps[:, bank, a:a + n], nFq[:, qb, ds(2 * (i - 1) + t, 1)],
                                            nFb[:, t, 0:n], ALU.subtract, ALU.add).then_inc(s_add, 1)
                    ve.wait_ge(s_add, 8 * (i - 1) + 4 * t + turn + 1)
                    ve.tensor_reduce(nmx[:, t, qb:qb + 1], pr, AX_X, ALU.max, negate=True).then_inc(s_max, 1)

            def probs_norm(i, t):
                ve.wait_ge(p_exp, 8 * (i - 1) + 4 * t + 4)
                ve.reciprocal(rsum[:, t], psum_row[:, t]).then_inc(p_rec, 1)
                ve.wait_ge(p_rec, 2 * (i - 1) + t + 1)
                for qb in range(NB):
                    pr = prob[:, t, P_AT[qb]:P_AT[qb] + P * (qb + 1)]
                    ve.tensor_scalar(pr, pr, rsum[:, t, qb:qb + 1], None, ALU.mult).then_inc(p_norm, 1)

            def probs_lo(i, t):
                for g, (bank, a, n, to) in enumerate(PT_EVAC):
                    ve.wait_ge(pt_hi, 6 * (i - 1) + 3 * t + g + 1)
                    ve.tensor_tensor(pt[:, LO, to:to + n], ps[:, bank, a:a + n],
                                     pt[:, HI, to:to + n].bitcast(F), ALU.subtract).then_inc(pt_lo, 1)

            def y_lo(i, t):
                ve.wait_ge(ya_hi, 2 * (i - 1) + t + 1)
                ve.tensor_tensor(yatt[:, LO, 2 * (i - 1) + t], ps[:, 7, :],
                                 yatt[:, HI, 2 * (i - 1) + t].bitcast(F), ALU.subtract).then_inc(ya_lo, 1)

            def att_step(i):
                scores_add(i, 0)
                lo(C_ATT, i, stride=4)
                probs_norm(i, 0)
                scores_add(i, 1)
                probs_norm(i, 1)
                lo(C_ATT + 1, i, stride=4)
                probs_lo(i, 0)
                qk_lo(i, 0, 0)
                y_lo(i, 0)
                probs_lo(i, 1)
                qk_lo(i, 1, 0)
                lo(C_ATT + 2, i, stride=4)
                y_lo(i, 1)
                qk_lo(i, 0, 1)
                qk_lo(i, 1, 1)
                lo(C_ATT + 3, i, stride=4)
                v_lo(i, 0)
                v_lo(i, 1)

            lo(C_ATT + 1)
            qk_lo(0, 0, 0)
            qk_lo(0, 1, 0)
            lo(C_ATT + 2)
            qk_lo(0, 0, 1)
            qk_lo(0, 1, 1)
            lo(C_ATT + 3)
            v_lo(0, 0)
            v_lo(0, 1)
            with ve.Fori(1, H // 2) as i:
                att_step(i)
            last = H // 2
            scores_add(last, 0)
            lo(C_PRA)
            probs_norm(last, 0)
            scores_add(last, 1)
            probs_norm(last, 1)
            probs_lo(last, 0)
            y_lo(last, 0)
            probs_lo(last, 1)
            y_lo(last, 1)

            for cc in range(4):
                lo(C_PRA + 1 + cc)
                ada(12 + cc)
                for t in range(2):
                    jt = 2 * cc + t
                    wait_from(ve, mb_lo, jt - 1)
                    if t == 0:
                        ve.wait_ge(tile0, first(C_PRA + cc))
                    else:
                        ve.wait_ge(w_used, whole(C_PRA + cc))
                    ve.wait_ge(siga_done, jt + 1)
                    ve.tensor_tensor(mt[:, t], ps[:, 2 * (cc % 2) + t, :], sig_a[:, jt], ALU.mult)\
                      .then_inc(mb_mul, 1)
                    ve.wait_ge(mb_mul, jt + 1)
                    ve.tensor_tensor(mt[:, t], mt[:, t], merged_a[:, jt], ALU.add).then_inc(mb_add, 1)
                for t in range(2):
                    jt = 2 * cc + t
                    ve.wait_ge(mb_hi, jt + 1)
                    ve.tensor_tensor(h[:, LO, jt], mt[:, t], h[:, HI, jt].bitcast(F), ALU.subtract)\
                      .then_inc(mb_lo, 1)
                ada_store(12 + cc)

            ve.wait_ge(ada_out, 16)
            ve.tensor_copy(fin_cols[:, 0:KD], mod[:, M_GT2:M_GT2 + KD]).then_inc(fin_done, 1)
            ve.scalar_tensor_tensor(fin_cols[:, KD:2 * KD], mod[:, M_SCF:M_SCF + KD], 1.0,
                                    vec[:, V_GF:V_GF + KD], ALU.add, ALU.mult).then_inc(fin_done, 1)
            ve.tensor_copy(fin_cols[:, 2 * KD:3 * KD], mod[:, M_SHF:M_SHF + KD]).then_inc(fin_done, 1)
            ve.scalar_tensor_tensor(gs2, mod[:, M_SC2:M_SC2 + KD], 1.0, vec[:, V_G2:V_G2 + KD],
                                    ALU.add, ALU.mult).then_inc(gs_done, 1)

            ve.wait_ge(xT_loaded, 16)
            for cc in range(4):
                lo(C_OUT + 1 + cc)
                for t in range(2):
                    jt = 2 * cc + t
                    if t == 0:
                        ve.wait_ge(tile0, first(C_OUT + cc))
                    else:
                        ve.wait_ge(w_used, whole(C_OUT + cc))
                    ve.scalar_tensor_tensor(x1T[:, jt], ps[:, 2 * (cc % 2) + t, :],
                                            mod[:, M_GT1 + jt:M_GT1 + jt + 1], x1T[:, jt],
                                            ALU.mult, ALU.add).then_inc(x1_done, 1)
                for t in range(2):
                    jt = 2 * cc + t
                    ve.wait_ge(sq_done, jt + 1)
                    if jt == 0:
                        ve.tensor_copy(sqacc[:, :], sq2[:, 0]).then_inc(sq_added, 1)
                    else:
                        ve.wait_ge(sq_added, jt)
                        ve.tensor_tensor(sqacc[:, :], sqacc[:, :], sq2[:, t], ALU.add).then_inc(sq_added, 1)
                if cc == 0:
                    ve.wait_ge(fin_mm, 1)
                    ve.tensor_copy(fin_rows[:, :], ps[0:3 * KD, 7, 0:P]).then_inc(fin_row, 1)

            ve.wait_ge(ms2_mm, 1)
            ve.tensor_scalar(ss2, ps[:, 2, 0:NB], 1.0 / D, EPS, ALU.mult, ALU.add).then_inc(ms2_mean, 1)
            ve.wait_ge(ms2_sqrt, 1)
            ve.reciprocal(rs2, rs2).then_inc(rs2_done, 1)
            ve.wait_ge(rs2_done, 1)
            for b in range(NB):
                ve.tensor_scalar(diag[:, P * b:P * b + P], ident[:, :], rs2[:, b:b + 1], None, ALU.mult)\
                  .then_inc(diag_done, 1)
            ve.wait_ge(rs2_mm, 1)
            ve.wait_ge(gs_done, 2)

            def h2_low(k):
                ve.wait_ge(h2_hi, k + 1)
                ve.scalar_tensor_tensor(h[:, LO, k], htmp2[:, k % 2], mod[:, M_SH2 + k:M_SH2 + k + 1],
                                        h[:, HI, k].bitcast(F), ALU.add, ALU.subtract).then_inc(h2_lo, 1)
            for k in range(KD):
                wait_from(ve, h2_lo, k - 1)
                ve.scalar_tensor_tensor(htmp2[:, k % 2], x1T[:, k], gs2[:, k:k + 1], ps[:, 3, :],
                                        ALU.mult, ALU.mult).then_inc(h2_tmp, 1)
                if k:
                    h2_low(k - 1)
            h2_low(KD - 1)

            def down_lo(c0, i=0):
                lo(c0, i)
                for u in range(2):
                    n = 2 * (c0 - C_DOWN) + u
                    sl = 2 * (c0 % 2) + u
                    ve.wait_ge(act_hi, n + 1 + 4 * i)
                    ve.tensor_tensor(act_s[:, sl, LO], act[:, n + 4 * i], act_s[:, sl, HI].bitcast(F),
                                     ALU.subtract).then_inc(act_lo, 1)

            def up_step(i, following):
                lo(C_UP + 1, i)
                for t in range(2):
                    ve.wait_ge(fconv0, 2 * i + t + 1)
                    for d in range(1, 3):
                        if d > 1:
                            ve.wait_ge(fconv_tap, 4 * i + 2 * t + d - 1)
                        ve.scalar_tensor_tensor(cv[:, t, d:T], ps[:, t, 0:T - d],
                                                vec[:, ds(V_FW + (2 - d) * NF + t + 2 * i, 1)],
                                                cv[:, t, d:T], ALU.mult, ALU.add).then_inc(fconv_tap, 1)
                following(i)
                for t in range(2):
                    ve.wait_ge(fgelu, 2 * i + t + 1)
                    if t == 0:
                        ve.wait_ge(tile0, first(C_UP + 1, i))
                    else:
                        ve.wait_ge(w_used, whole(C_UP + 1, i))
                    ve.tensor_tensor(act[:, 2 * i + t], gg[:, t], ps[:, 2 + t, :], ALU.mult)\
                      .then_inc(act_done, 1)

            up_step(0, lambda i: lo(C_UP + 2, i))
            with ve.Fori(1, NF // 2 - 1) as i:
                up_step(i, lambda i: lo(C_UP + 2, i))
            up_step(NF // 2 - 1, lambda i: down_lo(C_DOWN))
            with ve.Fori(0, NF // 4 - 1) as i:
                down_lo(C_DOWN + 1, i)
                down_lo(C_DOWN + 2, i)
            down_lo(C_END - 1)

            def gate_y(b):
                wait_from(ve, o_mul, b - 1)
                wait_from(ve, ms3_sum, b - 1)
                ve.wait_ge(down_mm, b + 1)
                ve.tensor_tensor(x2[:, b % 2], ps[:, 2 * b:2 * b + 2, :].rearrange("p a n -> p (a n)"),
                                 bc[:, 0], ALU.mult).then_inc(x2_mul, 1)
            ve.wait_ge(fin_loaded, 16)
            gate_y(0)
            for b in range(NB):
                if b + 1 < NB:
                    gate_y(b + 1)
                ve.wait_ge(ms3_sum, b + 1)
                ve.tensor_scalar(ss3[:, b:b + 1], ss3[:, b:b + 1], 1.0 / D, EPS, ALU.mult, ALU.add)\
                  .then_inc(ms3_mean, 1)
                ve.wait_ge(ms3_sqrt, b + 1)
                ve.reciprocal(rs3[:, b:b + 1], rs3[:, b:b + 1]).then_inc(rs3_done, 1)
                ve.wait_ge(rs3_done, b + 1)
                if b >= 2:
                    ve.wait_ge(out_stored[b % 2], 16)
                ve.scalar_tensor_tensor(o_nat[:, b % 2], x2[:, b % 2], rs3[:, b:b + 1], bc[:, 1],
                                        ALU.mult, ALU.mult).then_inc(o_mul, 1)

        @block.tensor
        def _(te):
            def mm3(dst, lhs, rhs, start, stop):
                te.matmul(dst, lhs(LO), rhs(HI), start=start, stop=False)
                te.matmul(dst, lhs(HI), rhs(LO), start=False, stop=False)
                return te.matmul(dst, lhs(HI), rhs(HI), start=False, stop=stop)

            def w_tile(s, k, t, n):
                return lambda part: wsplit[:, s, part, k * n + P * t:k * n + P * t + P]

            def features(x_, k):
                return lambda part: x_[:, part, k]

            def project(c0, x_, bank, t, n=256, kk=KD, ready=None):
                for k in range(kk):
                    if ready:
                        ready(k)
                    ins = mm3(ps[:, bank, :], w_tile(c0 % 2, k, t, n), features(x_, k), k == 0, k == kk - 1)
                return ins

            def project2(c0, x_, bank, ready):
                for k in range(KD):
                    ready(k)
                    for t in range(2):
                        ins = mm3(ps[:, bank + t, :], w_tile(c0 % 2, k, t, 256), features(x_, k),
                                  k == 0, k == KD - 1)
                        if k == KD - 1:
                            ins.then_inc(tile0 if t == 0 else w_used, 1)

            def ada_columns(idx):
                te.wait_ge(ada_part, 8 * idx + 8)
                wait_from(te, ada_out, idx)
                for j in range(4):
                    ins = te.matmul(ps[:, 6, j:j + 1], ada_acc[:, P * j:P * j + P], ones[:, 0:1],
                                    start=True, stop=True)
                ins.then_inc(ada_mm, 1)

            te.sem_inc(w_used, RING)
            te.wait_ge(consts, 6)
            te.wait_ge(vec_loaded, 16 * 13)
            te.transpose(ps[:, 0, 0:V_ROWS_A], vrows[0:V_ROWS_A, 0], ident[0:V_ROWS_A, 0:V_ROWS_A])
            nb_, nc_ = V_ROWS_B - V_ROWS_A, V_END - V_ROWS_B
            te.transpose(ps[:, 0, V_ROWS_A:V_ROWS_B], vrows[0:nb_, 1], ident[0:nb_, 0:nb_])
            te.transpose(ps[:, 0, V_ROWS_B:V_END], vrows[0:nc_, 2], ident[0:nc_, 0:nc_]).then_inc(vec_mm, 1)
            ada_columns(0)
            ada_columns(1)
            for b in range(NB):
                te.wait_ge(x_loaded[b], 16)
            for k in range(KD):
                if k >= 4:
                    te.wait_ge(xT_copied, k - 3)
                for b in range(NB):
                    ins = te.transpose(ps[:, 2 + k % 4, P * b:P * b + P], x_nat[:, b, P * k:P * k + P],
                                       ident[:, :])
                ins.then_inc(xT_mm, 1)

            def xs_transposes(k):
                if k < 4:
                    te.wait_ge(xT_copied, k + 5)
                else:
                    te.wait_ge(h_tmp, k - 3)
                for b in range(NB):
                    ins = te.transpose(ps[:, 2 + k % 4, P * b:P * b + P], xs_nat[:, b, P * k:P * k + P],
                                       ident[:, :])
                ins.then_inc(xsT_mm, 1)
            te.wait_ge(xs_done, NB)
            for k in range(4):
                xs_transposes(k)
            ada_columns(2)
            ada_columns(3)
            for k in range(4, KD):
                xs_transposes(k)

            def rnn_gates(i):
                te.wait_ge(lru_lo, 2 + i)
                wait_from(te, sig_done, 4 * i)
                for t in range(2):
                    te.wait_ge(xr_part, 4 * i + 2 * t + 2)
                    for g in range(2):
                        mm3(ps[:, 4 + 2 * g + t, :], lambda part: lru_w[:, part, g, t],
                            lambda part: xrs[:, t, part], True, True).then_inc(gate_mm, 1)

            def rnn_step(i, peeled=False):
                te.wait_ge(w_lo, whole(C_RNN, i))
                if peeled:
                    project2(C_RNN, h, 0, lambda k: te.wait_ge(h_lo, k + 1))
                else:
                    te.wait_ge(conv_tap, 6 * i)
                    project(C_RNN, h, 0, 0).then_inc(tile0, 1)
                    project(C_RNN, h, 1, 1).then_inc(w_used, 1)
                te.wait_ge(w_lo, whole(C_RNN + 1, i))
                wait_from(te, gelu_done, 2 * i)
                project(C_RNN + 1, h, 2, 0).then_inc(tile0, 1)
                project(C_RNN + 1, h, 3, 1).then_inc(w_used, 1)
                rnn_gates(i)

            rnn_step(0, peeled=True)
            with te.Fori(1, NR // 2) as i:
                rnn_step(i)

            def mix_step(j, gate=None, y_ready=None):
                te.wait_ge(w_lo, whole(C_MIX, j))
                if gate:
                    te.wait_ge(conv_tap, 3 * NR)
                else:
                    te.wait_ge(sigr_done, j)
                project(C_MIX, h, 0, 0, P).then_inc(w_used, 1)
                if gate:
                    gate()
                te.wait_ge(w_lo, whole(C_MIX + 1, j))
                if not gate:
                    te.wait_ge(mixa_done, j)
                project(C_MIX + 1, yrnn, 2, 0, P, NR, y_ready).then_inc(w_used, 1)
                ada_columns(4 + j)

            def forget_gate():
                te.wait_ge(fw_lo, 1)
                for k in range(KD):
                    ins = mm3(ps[0:H, 1, :], lambda part: fws[:, part, k], features(h, k), k == 0, k == KD - 1)
                ins.then_inc(fl_mm, 1)
                te.wait_ge(gelu_done, NR)
            mix_step(0, forget_gate, lambda k: te.wait_ge(y_part, 2 * k + 2))
            with te.Fori(1, KD) as j:
                mix_step(j)
            te.wait_ge(fl_step, 6)
            for b in range(NB):
                ins = te.transpose(ps[:, 1, H * b:H * b + H], nF[:, P * b:P * b + P], ident[0:H, 0:H])
            ins.then_inc(nFq_mm, 1)

            def qk_proj(i, which, t):
                c0 = C_ATT + which
                if t == 0:
                    te.wait_ge(w_lo, whole(c0, i, 4))
                project(c0, h, t, t).then_inc(tile0 if t == 0 else w_used, 1)

            def v_proj(i):
                te.wait_ge(w_lo, whole(C_ATT + 2, i, 4))
                s = C_ATT % 2
                for b in range(NB):
                    if b % 2 == 0:
                        te.wait_ge(att_lo, 3 + b // 2 + 6 * i)
                    for k in range(KD):
                        ins = mm3(ps[:, b // 2, 256 * (b % 2):256 * (b % 2) + 256],
                                  lambda part: h[:, part, k, P * b:P * b + P],
                                  lambda part: wsplit[:, s, part, 256 * k:256 * k + 256], k == 0, k == KD - 1)
                    if b == 1:
                        ins.then_inc(tile0, 1)
                ins.then_inc(w_used, 1)

            def gate_proj(i, t):
                if t == 0:
                    te.wait_ge(w_lo, whole(C_ATT - 1, i, 4))
                te.wait_ge(att_lo, 6 * (i - 1) + 5 + t)
                project(C_ATT - 1, h, t, t).then_inc(tile0 if t == 0 else w_used, 1)

            def scores(i, t):
                te.wait_ge(att_lo, 6 * (i - 1) + 4)
                if t == 1:
                    te.wait_ge(s_add, 8 * (i - 1) + 4)
                for qb in S_ORDER:
                    n = P * (qb + 1)
                    bank, a = S_AT[qb]
                    mm3(ps[:, bank, a:a + n], lambda part: qk[:, t, 0, part, P * qb:P * qb + P],
                        lambda part: qk[:, t, 1, part, 0:n], True, False)
                    te.matmul(ps[:, bank, a + n - P:a + n], identb[:, :], maskb[:, :], start=False, stop=True)\
                      .then_inc(s_mm, 1)

            def prob_transposes(i, t):
                te.wait_ge(p_norm, 8 * (i - 1) + 4 * t + 4)
                for kbs in ((0,), (1, 3), (2,)):
                    if kbs == (2,) and t == 0:
                        te.wait_ge(s_add, 8 * (i - 1) + 8)
                    for kb in kbs:
                        bank, a, _ = PT_AT[kb]
                        for qb in range(kb, NB):
                            at_ = a + P * (qb - kb)
                            pcol = P_AT[qb] + P * kb
                            ins = te.transpose(ps[:, bank, at_:at_ + P], prob[:, t, pcol:pcol + P], ident[:, :])
                    ins.then_inc(t_mm, 1)

            def weighted(i, t):
                te.wait_ge(pt_lo, 6 * (i - 1) + 3 * t + 3)
                if t == 1:
                    te.wait_ge(ya_lo, 2 * (i - 1) + 1)
                for kb in range(NB):
                    n = T - P * kb
                    a = PT_AT[kb][2]
                    ins = mm3(ps[:, 7, P * kb:T], lambda part: vh[:, part, kb, P * t:P * t + P],
                              lambda part: pt[:, part, a:a + n], kb == 0, kb == NB - 1)
                ins.then_inc(pv_mm, 1)

            def att_step(i):
                scores(i, 0)
                gate_proj(i, 0)
                scores(i, 1)
                gate_proj(i, 1)
                prob_transposes(i, 0)
                te.wait_ge(siga_done, 2 * (i - 1) + 1)
                qk_proj(i, 0, 0)
                weighted(i, 0)
                prob_transposes(i, 1)
                te.wait_ge(siga_done, 2 * (i - 1) + 2)
                qk_proj(i, 0, 1)
                weighted(i, 1)
                te.wait_ge(att_lo, 6 * i + 1)
                qk_proj(i, 1, 0)
                te.wait_ge(att_lo, 6 * i + 2)
                qk_proj(i, 1, 1)
                v_proj(i)

            te.wait_ge(sigr_done, KD)
            qk_proj(0, 0, 0)
            te.wait_ge(fl_step, 7)
            qk_proj(0, 0, 1)
            te.wait_ge(att_lo, 1)
            qk_proj(0, 1, 0)
            te.wait_ge(att_lo, 2)
            qk_proj(0, 1, 1)
            v_proj(0)
            with te.Fori(1, H // 2) as i:
                att_step(i)
            last = H // 2
            scores(last, 0)
            gate_proj(last, 0)
            scores(last, 1)
            gate_proj(last, 1)
            prob_transposes(last, 0)
            weighted(last, 0)
            prob_transposes(last, 1)
            weighted(last, 1)

            for cc in range(4):
                te.wait_ge(w_lo, whole(C_PRA + cc))
                for t in range(2):
                    jt = 2 * cc + t
                    bank = 2 * (cc % 2) + t
                    if cc == 0:
                        te.wait_ge(siga_done, KD - 1 + t)
                    elif cc == 1:
                        te.wait_ge(s_add, 4 * H)
                    else:
                        te.wait_ge(mb_mul, jt - 3)
                    project(C_PRA + cc, yatt, bank, t, ready=(lambda k: te.wait_ge(ya_lo, k + 1)) if jt == 0 else None)\
                        .then_inc(tile0 if t == 0 else w_used, 1)
                ada_columns(12 + cc)

            te.wait_ge(fin_done, 3)
            te.transpose(ps[0:3 * KD, 7, 0:P], fin_cols[:, :], ident[:, :]).then_inc(fin_mm, 1)

            def x1_transposes(half):
                for b in range(NB):
                    for j in range(4):
                        ins = te.transpose(ps[:, 4 + b, P * j:P * j + P], x1T[:, 4 * half + j, P * b:P * b + P],
                                           ident[:, :])
                    ins.then_inc(x1n_mm, 1)
            for cc in range(4):
                te.wait_ge(w_lo, whole(C_OUT + cc))
                for t in range(2):
                    jt = 2 * cc + t
                    bank = 2 * (cc % 2) + t
                    if cc < 2:
                        te.wait_ge(mb_mul, 5 + jt)
                    else:
                        te.wait_ge(x1_done, jt - 3)
                    project(C_OUT + cc, h, bank, t, ready=(lambda k: te.wait_ge(mb_lo, k + 1)) if jt == 0 else None)\
                        .then_inc(tile0 if t == 0 else w_used, 1)
                    if jt == 4:
                        te.wait_ge(x1_done, 4)
                        te.wait_ge(fin_row, 1)
                        x1_transposes(0)
            te.wait_ge(sq_added, KD)
            for b in range(NB):
                ins = te.matmul(ps[:, 2, b:b + 1], sqacc[:, P * b:P * b + P], ones[:, 0:1], start=True, stop=True)
            ins.then_inc(ms2_mm, 1)
            te.wait_ge(x1n_done, 4)
            x1_transposes(1)
            te.wait_ge(diag_done, NB)
            te.matmul(ps[:, 3, :], ones[:, :], diag[:, :], start=True, stop=True).then_inc(rs2_mm, 1)

            def up_step(i, peeled=False):
                te.wait_ge(w_lo, whole(C_UP, i))
                if peeled:
                    project2(C_UP, h, 0, lambda k: te.wait_ge(h2_lo, k + 1))
                else:
                    te.wait_ge(fconv_tap, 4 * i)
                    project(C_UP, h, 0, 0).then_inc(tile0, 1)
                    project(C_UP, h, 1, 1).then_inc(w_used, 1)
                te.wait_ge(w_lo, whole(C_UP + 1, i))
                wait_from(te, act_done, 2 * i)
                project(C_UP + 1, h, 2, 0).then_inc(tile0, 1)
                project(C_UP + 1, h, 3, 1).then_inc(w_used, 1)

            up_step(0, peeled=True)
            with te.Fori(1, NF // 2) as i:
                up_step(i)

            def down_block(s, u, b, start, stop):
                for half in range(2):
                    ins = mm3(ps[:, 2 * b + half, :], lambda part: act_s[:, 2 * s + u, part, P * b:P * b + P],
                              lambda part: wsplit[:, s, part, D * u + T * half:D * u + T * half + T], start, stop)
                return ins

            def down_chunk(c0, i=0, start=False):
                te.wait_ge(w_lo, whole(c0, i))
                te.wait_ge(act_lo, 2 * (c0 - C_DOWN) + 2 + 4 * i)
                for u in range(2):
                    for b in (2, 3, 0, 1):
                        if start and u == 0 and b == 2:
                            te.wait_ge(x1n_done, 2 * NB)
                        if start and u == 0 and b == 0:
                            te.wait_ge(act_done, NF)
                        ins = down_block(c0 % 2, u, b, start and u == 0, False)
                ins.then_inc(w_used, 1)

            down_chunk(C_DOWN, start=True)
            down_chunk(C_DOWN + 1)
            with te.Fori(1, NF // 4 - 1) as i:
                down_chunk(C_DOWN, i)
                down_chunk(C_DOWN + 1, i)
            down_chunk(C_END - 2)
            te.wait_ge(w_lo, whole(C_END - 1))
            te.wait_ge(act_lo, NF)
            for b in range(NB):
                down_block(1, 0, b, False, False)
                down_block(1, 1, b, False, True).then_inc(down_mm, 1)


INPUTS = ["x", "c", "w_ada", "b_ada", "g_norm1", "w_in", "w_rnn_conv", "b_rnn_conv", "w_lru_a", "b_lru_a",
          "w_lru_i", "b_lru_i", "lru_lambda", "b_fgate", "w_proj_rnn", "w_proj_attn", "w_out", "g_norm2",
          "w_ffn_up", "w_ffn_conv", "b_ffn_conv", "w_ffn_down", "w_ada_final", "b_ada_final", "g_final"]


def kernel(**inputs):
    import numpy as np
    import concourse.bacc as bacc
    from concourse.bass_utils import run_bass_kernel_spmd

    nc = bacc.Bacc("TRN2", target_bir_lowering=False, num_devices=1)
    arrays, args = {}, []
    for name in INPUTS:
        a = np.ascontiguousarray(inputs[name])
        arrays[f"in_{name}"] = a
        args.append(nc.dram_tensor(f"in_{name}", a.shape, mybir.dt.from_np(a.dtype), kind="ExternalInput").ap())
    args.append(nc.dram_tensor("out_x", (1, T, D), FP32, kind="ExternalOutput").ap())
    hybrid_block(nc, *args)
    r = run_bass_kernel_spmd(nc, [arrays], core_ids=[0])
    return r.results[0]["out_x"]
```

```python
import concourse.bass as bass
from concourse import mybir
from contextlib import ExitStack

FP32 = mybir.dt.float32
F32R = mybir.dt.float32r
BF16 = mybir.dt.bfloat16
ACT = mybir.ActivationFunctionType
ALU = mybir.AluOpType
AX_X = mybir.AxisListType.X
ds = bass.ds

P = 128
T = 512
NB = T // P
D = 1024
KD = D // P
DR = 1280
NR = DR // P
H = 8
DFF = 3 * D
NF = DFF // P
EPS = 1e-6
LRU_C = 8.0
MASKED = -1e30
RING = 2
ARENA_KB = 206

COL_XR, COL_GR = 0, DR
COL_Q = 2 * DR
COL_K, COL_V = COL_Q + D, COL_Q + 2 * D
COL_FL = COL_Q + 3 * D
COL_MR = COL_FL + H
COL_MA = COL_MR + D

C_RNN = 0
C_MIX = C_RNN + NR
C_ATT = C_MIX + 2 * KD
C_PRA = C_ATT + 4 * H // 2
C_OUT = C_PRA + KD // 2
C_UP = C_OUT + KD // 2
C_DOWN = C_UP + NF
C_END = C_DOWN + NF // 2

V_BADA = 0
V_G1 = V_BADA + 5 * KD
V_CW = V_G1 + KD
V_ROWS_A = V_CW + 4 * NR
V_CB = V_ROWS_A
V_BA, V_BI, V_LAM = V_CB + NR, V_CB + 2 * NR, V_CB + 3 * NR
V_G2 = V_LAM + NR
V_ROWS_B = V_G2 + KD
V_FW = V_ROWS_B
V_FB = V_FW + 3 * NF
V_END = V_FB + NF

M_SH1, M_SC1, M_GT1, M_SH2, M_SC2 = (KD * v for v in range(5))
N_COLS, N_START = 10, 4


def hybrid_block(nc, x, c, w_ada, b_ada, g_norm1, w_in, w_rnn_conv, b_rnn_conv, w_lru_a, b_lru_a,
                 w_lru_i, b_lru_i, lru_lambda, b_fgate, w_proj_rnn, w_proj_attn, w_out, g_norm2,
                 w_ffn_up, w_ffn_conv, b_ffn_conv, w_ffn_down, w_ada_final, b_ada_final, g_final,
                 out):
    ctx = ExitStack()
    with ctx:
        def sem(name):
            return ctx.enter_context(nc.semaphore(name))

        KB = 1024
        base = -(-nc.sbuf_base // 32) * 32
        ctx.enter_context(nc.sbuf_tensor("arena", [P, ARENA_KB * KB // 4], FP32))

        def at(name, kb, shape, dtype=FP32):
            return nc.alloc_sbuf_tensor_at(name, shape, dtype, offset=base + int(kb * KB))

        HI, LO = 0, 1
        h = at("h", 0, [P, 2, KD, T], F32R)
        wsplit = at("wsplit", 32, [P, RING, 2, 2048], F32R)
        wraw = at("wraw", 64, [P, RING, 2048])
        yrnn = at("yrnn", 80, [P, 2, NR, T], F32R)
        qk = at("qk", 80, [P, 2, 2, 2, T], F32R)
        sig_a = at("sig_a", 96, [P, KD, T])
        x1T = at("x1T", 80, [P, KD, T])
        act = at("act", 80, [P, NF, T])
        x_nat = at("x_nat", 112, [P, NB, D])
        xT_out = at("xT_out", 80, [P, KD, T])
        yatt = at("yatt", 112, [P, 2, H, T], F32R)
        x1_nat = at("x1_nat", 128, [P, NB, D])
        rg = at("rg", 120, [P, 2, T])
        ig = at("ig", 124, [P, 2, T])
        av = at("av", 128, [P, 2, T])
        ev = at("ev", 132, [P, 2, T])
        th = at("th", 136, [P, 2, T])
        gl = at("gl", 140, [P, 2, T])
        xc = at("xc", 144, [P, 2, T])
        xrs = at("xrs", 148, [P, 2, 2, T], F32R)
        lru_raw = at("lru_raw", 156, [P, 2, 2, P])
        lru_w = at("lru_w", 180, [P, 2, 2, 2, P], F32R)
        sq1 = at("sq1", 96, [P, NB, D])
        ada_first = at("ada_first", 128, [P, 6, 4, T])
        ada_raw = at("ada_raw", 160, [P, 2, 4, T])
        ada_acc = at("ada_acc", 176, [P, T])
        ada_split = at("ada_split", 194, [P, 2, T], F32R)
        ada_diag = at("ada_diag", 178, [P, T])
        htmp = at("htmp", 180, [P, 2, T])
        diag1 = at("diag1", 184, [P, T])
        cact_rows = at("cact_rows", 188, [P, KD, P])
        merged_a = at("merged_a", 144, [P, KD, T])
        pt = at("pt", 160, [P, 2, 1280], F32R)
        vh = at("vh", 170, [P, 2, NB, 2 * P], F32R)
        prob = at("prob", 178, [P, 2, 1280])
        nFb = at("nFb", 188, [P, 2, T])
        mt = at("mt", 180, [P, 2, T])
        sq2 = at("sq2", 178, [P, 2, T])
        sqacc = at("sqacc", 182, [P, T])
        diag = at("diag", 184, [P, T])
        htmp2 = at("htmp2", 186, [P, 2, T])
        cv = at("cv", 144, [P, 2, T])
        gg = at("gg", 148, [P, 2, T])
        act_s = at("act_s", 160, [P, 4, 2, T], F32R)
        sqe = at("sqe", 144, [P, NB, 2, T])
        bc = at("bc", 178, [P, 3, D])
        g_rows = at("g_rows", 190, [P, D])
        o_nat = at("o_nat", 80, [P, NB, D])
        x2 = at("x2", 96, [P, NB, D])
        nF = at("nF", 192, [H, T])
        fl1 = at("fl1", 194, [H, T])
        fl2 = at("fl2", 196, [H, T])
        onesrow = at("onesrow", 198, [H, T])
        vrows = at("vrows", 192, [P, 3, P])
        ident = at("ident", 200, [P, P])
        ones = at("ones", 200.5, [P, P])
        identb = at("identb", 201, [P, P], BF16)
        maskb = at("maskb", 201.25, [P, P], BF16)
        vec = at("vec", 201.5, [P, V_END])
        mod = at("mod", 203, [P, 5 * KD])
        fw = at("fw", 203.25, [P, KD, H])
        fws = at("fws", 203.5, [P, 2, KD, H], F32R)
        nFq = at("nFq", 204, [P, NB, H])
        bfg = at("bfg", 204.125, [H, 1])
        small = at("small", 204.25, [P, 160])

        def cols(a, n):
            return small[:, a:a + n]
        cact, csig, ccol = cols(0, KD), cols(8, KD), cols(152, KD)
        gs1 = cols(16, KD)
        gs2 = cols(24, KD)
        ss1, rs1 = cols(32, NB), cols(36, NB)
        ss2, rs2 = cols(40, NB), cols(44, NB)
        ms3, rs3 = cols(48, NB), cols(52, NB)
        lam_a, lam_e, lam_t, lam_u, lam_p = (cols(56 + NR * j, NR) for j in range(5))
        sp_m8, sp_p4 = cols(106, NR), cols(116, NR)
        ss3 = cols(136, 2 * NB)
        newton_t = cols(126, NB)
        nmx = at("nmx", 205.125, [P, 2, NB])
        psum_row = at("psum_row", 205.25, [P, 2, NB])
        rsum = at("rsum", 205.375, [P, 2, NB])
        ones_r = at("ones_r", 205.5, [P, P], F32R)

        ps = ctx.enter_context(nc.psum_tensor("ps", [P, 8, T], FP32))

        xT_dram = nc.dram_tensor("xT_dram", [P, KD, T], FP32).ap()
        nF_dram = nc.dram_tensor("nF_dram", [H, T], FP32).ap()

        w_in_v = w_in[0].rearrange("(k p) n -> p k n", p=P)
        w_ada_v = w_ada[0].rearrange("(k p) n -> p k n", p=P)
        w_adf_v = w_ada_final.rearrange("(k p) n -> p k n", p=P)
        w_pr_v = w_proj_rnn[0].rearrange("(k p) n -> p k n", p=P)
        w_pa_v = w_proj_attn[0].rearrange("(k p) n -> p k n", p=P)
        w_out_v = w_out[0].rearrange("(k p) n -> p k n", p=P)
        w_up_v = w_ffn_up[0].rearrange("(k p) n -> p k n", p=P)
        w_dn_v = w_ffn_down[0].rearrange("(k p) n -> p k n", p=P)
        w_la_v = w_lru_a[0].rearrange("n c d -> c n d")
        w_li_v = w_lru_i[0].rearrange("n c d -> c n d")
        x_v = x[0].rearrange("(b p) d -> p b d", p=P)
        out_v = out[0].rearrange("(b p) d -> p b d", p=P)

        vec_loaded = sem("vec_loaded")
        vec_a_loaded = sem("vec_a_loaded")
        small_loaded = sem("small_loaded")
        x_loaded = [sem(f"x_loaded{b}") for b in range(NB)]
        w_loaded = [sem(f"w_loaded{s}") for s in range(RING)]
        c_loaded = sem("c_loaded")
        ada_first_loaded = [sem(f"ada_first_loaded{n}") for n in range(2 * N_START)]
        ada_loaded = [sem(f"ada_loaded{s}") for s in range(2)]
        lru_loaded = sem("lru_loaded")
        xT_stored = sem("xT_stored")
        xT_loaded = sem("xT_loaded")
        nF_stored = sem("nF_stored")
        nF_loaded = sem("nF_loaded")
        bc_loaded = sem("bc_loaded")
        out_stored = sem("out_stored")
        w_hi = sem("w_hi")
        w_lo = sem("w_lo")
        w_used = sem("w_used")
        tile0 = sem("tile0")
        newton_step = sem("newton_step")
        consts = sem("consts")
        vec_mm = sem("vec_mm")
        vec_ok = sem("vec_ok")
        cact_row = sem("cact_row")
        csig_done = sem("csig_done")
        cact_done = sem("cact_done")
        lam_step = sem("lam_step")
        lam_exp = sem("lam_exp")
        ms1_sum = sem("ms1_sum")
        ms1_mean = sem("ms1_mean")
        ms1_sqrt = sem("ms1_sqrt")
        rs1_done = sem("rs1_done")
        diag1_done = sem("diag1_done")
        rs1_mm = sem("rs1_mm")
        xT_mm = sem("xT_mm")
        xT_copied = sem("xT_copied")
        gs_done = sem("gs_done")
        h_tmp = sem("h_tmp")
        h_hi = sem("h_hi")
        h_lo = sem("h_lo")
        ada_part = sem("ada_part")
        ada_hl = sem("ada_hl")
        ada_mm = sem("ada_mm")
        ada_pick = sem("ada_pick")
        ada_sum = sem("ada_sum")
        ada_out = sem("ada_out")
        fw_hi = sem("fw_hi")
        fw_lo = sem("fw_lo")
        fl_mm = sem("fl_mm")
        fl_step = sem("fl_step")
        fl_act = sem("fl_act")
        nFq_mm = sem("nFq_mm")
        gelu_done = sem("gelu_done")
        sig_done = sem("sig_done")
        exp_done = sem("exp_done")
        conv0 = sem("conv0")
        conv_tap = sem("conv_tap")
        xr_part = sem("xr_part")
        lru_hi = sem("lru_hi")
        lru_lo = sem("lru_lo")
        gate_mm = sem("gate_mm")
        ix_done = sem("ix_done")
        na_done = sem("na_done")
        a_done = sem("a_done")
        q_done = sem("q_done")
        sqrt_done = sem("sqrt_done")
        u_done = sem("u_done")
        scan_done = sem("scan_done")
        y_done = sem("y_done")
        y_part = sem("y_part")
        sigr_done = sem("sigr_done")
        mixa_done = sem("mixa_done")
        siga_done = sem("siga_done")
        att_hi = sem("att_hi")
        att_lo = sem("att_lo")
        s_mm = sem("s_mm")
        s_add = sem("s_add")
        s_max = sem("s_max")
        p_exp = sem("p_exp")
        p_rec = sem("p_rec")
        p_norm = sem("p_norm")
        t_mm = sem("t_mm")
        pt_hi = sem("pt_hi")
        pt_lo = sem("pt_lo")
        pv_mm = sem("pv_mm")
        ya_hi = sem("ya_hi")
        ya_lo = sem("ya_lo")
        mb_mul = sem("mb_mul")
        mb_add = sem("mb_add")
        mb_hi = sem("mb_hi")
        mb_lo = sem("mb_lo")
        bc_done = sem("bc_done")
        x1_done = sem("x1_done")
        sq_done = sem("sq_done")
        sq_added = sem("sq_added")
        x1n_mm = sem("x1n_mm")
        x1n_done = sem("x1n_done")
        ms2_mm = sem("ms2_mm")
        ms2_mean = sem("ms2_mean")
        ms2_sqrt = sem("ms2_sqrt")
        rs2_done = sem("rs2_done")
        diag_done = sem("diag_done")
        rs2_mm = sem("rs2_mm")
        h2_tmp = sem("h2_tmp")
        h2_hi = sem("h2_hi")
        h2_lo = sem("h2_lo")
        fconv0 = sem("fconv0")
        fconv_tap = sem("fconv_tap")
        fgelu = sem("fgelu")
        act_done = sem("act_done")
        act_hi = sem("act_hi")
        act_lo = sem("act_lo")
        down_mm = sem("down_mm")
        x2_mul = sem("x2_mul")
        x2_add = sem("x2_add")
        x2_add1 = sem("x2_add1")
        x2_last = sem("x2_last")
        ms3_sum = sem("ms3_sum")
        ms3_mean = sem("ms3_mean")
        ms3_sqrt = sem("ms3_sqrt")
        rs3_done = sem("rs3_done")
        o_mul = sem("o_mul")
        o_add = sem("o_add")
        o_last = sem("o_last")

        def landed(c0, i=0, stride=2):
            return 16 * (c0 // 2 + 1) + 8 * stride * i

        def whole(c0, i=0, stride=2):
            return c0 + RING + 1 + stride * i

        def first(c0, i=0, stride=2):
            return c0 + 1 - (2 * KD if c0 >= C_ATT - 4 else 0) + stride * i

        def wait_from(eng, s, value):
            if not isinstance(value, int) or value > 0:
                eng.wait_ge(s, value)

        S_AT = [(2, 0), (4, 0), (2, P), (3, 0)]
        S_ORDER = (0, 2, 3, 1)
        S_READY = (2, 2, 3, 4)
        P_AT = [0, P, 3 * P, 6 * P]
        PT_EVAC = [(5, 0, 4 * P, 0), (6, 0, 4 * P, 4 * P), (4, 2 * P, 2 * P, 8 * P)]
        PT_AT = {0: (5, 0, 0), 1: (6, 0, 4 * P), 3: (6, 3 * P, 7 * P), 2: (4, 2 * P, 8 * P)}
        SCALE = float(P) ** -0.5
        ADA_FIRST = 12
        LAM_STEPS = 25

        block = ctx.enter_context(nc.Block())

        @block.sync
        def _(sp):
            def load(c0, i, src, k, n, stride=2):
                s = c0 % 2
                sp.wait_ge(w_lo, c0 + 1 + stride * i)
                sp.dma_start(wraw[:, s, 0:k * n].rearrange("p (k n) -> p k n", k=k), src)\
                  .then_inc(w_loaded[s], 16)

            def load_ada(idx, src):
                for s in range(2):
                    sp.wait_ge(ada_part, 8 * (idx - N_START) + ADA_FIRST + 4 * s - 4)
                    sp.dma_start(ada_raw[:, s], src[:, 4 * s:4 * s + 4, :]).then_inc(ada_loaded[s], 16)

            def cols_of(v, col, n):
                return v[:, :, ds(col, n)]

            def load_first(n):
                if n >= 6:
                    sp.wait_ge(ada_mm, 1)
                sp.dma_start(ada_first[:, n % 6],
                             cols_of(w_ada_v, T * (n // 2), T)[:, 4 * (n % 2):4 * (n % 2) + 4, :])\
                  .then_inc(ada_first_loaded[n], 16)

            sp.dma_start(ccol, c[0].rearrange("(k p) -> p k", p=P), allow_slow_non_contiguous=True)\
              .then_inc(c_loaded, 16)
            load_first(0)
            load_first(1)
            for b in range(NB):
                sp.dma_start(x_nat[:, b], x_v[:, b]).then_inc(x_loaded[b], 16)
            for n in range(2, 6):
                load_first(n)
            load_first(6)
            load_first(7)
            load(C_RNN, 0, cols_of(w_in_v, COL_XR, 256), KD, 256)
            load(C_RNN + 1, 0, cols_of(w_in_v, COL_GR, 256), KD, 256)

            def load_lru(blocks):
                sp.dma_start(lru_raw[:, 0], w_la_v[:, blocks, :]).then_inc(lru_loaded, 16)
                sp.dma_start(lru_raw[:, 1], w_li_v[:, blocks, :]).then_inc(lru_loaded, 16)
            sp.wait_ge(ada_mm, 2)
            load_lru(ds(0, 2))

            with sp.Fori(1, NR // 2) as i:
                load(C_RNN, i, cols_of(w_in_v, COL_XR + 256 * i, 256), KD, 256)
                load(C_RNN + 1, i, cols_of(w_in_v, COL_GR + 256 * i, 256), KD, 256)
                sp.wait_ge(lru_lo, 1 + i)
                load_lru(ds(2 * i, 2))

            load(C_MIX, 0, cols_of(w_in_v, COL_MR, P), KD, P)
            load(C_MIX + 1, 0, cols_of(w_in_v, COL_MR + P, P), KD, P)
            with sp.Fori(0, KD - 2) as j:
                load(C_MIX + 2, j, cols_of(w_pr_v, P * j, P), NR, P)
                load(C_MIX + 3, j, cols_of(w_in_v, COL_MR + 2 * P + P * j, P), KD, P)
                load_ada(4 + j, cols_of(w_ada_v, 4 * T + T * j, T))
            load(C_MIX + 14, 0, cols_of(w_pr_v, 6 * P, P), NR, P)
            load(C_MIX + 15, 0, cols_of(w_pr_v, 7 * P, P), NR, P)

            def load_nF(i4):
                row = nF_dram.rearrange("(a h) t -> a (h t)", a=1)[:, ds(i4 * (T // 2), 2 * T)]
                sp.dma_start(nFb[:, :, :].rearrange("p h t -> p (h t)"), row.broadcast_to([P, 2 * T]))\
                  .then_inc(nF_loaded, 16)

            load(C_ATT, 0, cols_of(w_in_v, COL_Q, 256), KD, 256)
            load(C_ATT + 1, 0, cols_of(w_in_v, COL_K, 256), KD, 256)
            load(C_ATT + 2, 0, cols_of(w_in_v, COL_V, 256), KD, 256)
            sp.wait_ge(fl_step, 6)
            sp.dma_start(nF_dram, nF[:, :]).then_inc(nF_stored, 16)
            sp.wait_ge(nF_stored, 16)
            load_nF(0)
            with sp.Fori(4, 2 * H - 3, 4) as i4:
                load(C_ATT - 1, i4, cols_of(w_in_v, COL_MA - 256 + 64 * i4, 256), KD, 256, 1)
                load(C_ATT, i4, cols_of(w_in_v, COL_Q + 64 * i4, 256), KD, 256, 1)
                load(C_ATT + 1, i4, cols_of(w_in_v, COL_K + 64 * i4, 256), KD, 256, 1)
                load(C_ATT + 2, i4, cols_of(w_in_v, COL_V + 64 * i4, 256), KD, 256, 1)
                sp.wait_ge(s_add, 2 * i4)
                load_nF(i4)
            load(C_PRA - 1, 0, cols_of(w_in_v, COL_MA + 768, 256), KD, 256)

            for cc in range(4):
                load(C_PRA + cc, 0, cols_of(w_pa_v, 256 * cc, 256), KD, 256)
            sp.wait_ge(pv_mm, H)
            sp.wait_ge(xT_stored, 16)
            sp.dma_start(x1T[:, :, :], xT_dram).then_inc(xT_loaded, 16)
            for cc in range(4):
                load(C_OUT + cc, 0, cols_of(w_out_v, 256 * cc, 256), KD, 256)

            def load_up(i):
                load(C_UP, i, cols_of(w_up_v, 256 * i, 256), KD, 256)
                load(C_UP + 1, i, cols_of(w_up_v, DFF + 256 * i, 256), KD, 256)
            load_up(0)
            for idx in range(10, 12):
                load_up(idx - 9)
                load_ada(idx, cols_of(w_ada_v, T * idx, T))
            with sp.Fori(3, 7) as i:
                load_up(i)
                load_ada(9 + i, cols_of(w_adf_v, T * i - 3 * T, T))
            with sp.Fori(7, NF // 2) as i:
                load_up(i)
            with sp.Fori(0, NF // 4) as i:
                rows_of = w_dn_v[:, ds(4 * i, 4), :]
                load(C_DOWN, i, rows_of[:, 0:2], 2, D)
                load(C_DOWN + 1, i, rows_of[:, 2:4], 2, D)
            for b in range(NB):
                for half in range(2):
                    if b == NB - 1 and half == 1:
                        sp.wait_ge(o_last, 1)
                    else:
                        sp.wait_ge(o_add, 2 * b + half + 1)
                    cs = slice(T * half, T * half + T)
                    sp.dma_start(out_v[:, b, cs], o_nat[:, b, cs]).then_inc(out_stored, 16)
            sp.wait_ge(out_stored, 16 * 2 * NB)

        @block.gpsimd
        def _(pool):
            pool.memset(ident[:, :], 0.0).then_inc(consts, 1)
            pool.memset(maskb[:, :], 0.0).then_inc(consts, 1)
            pool.wait_ge(consts, 2)
            pool.affine_select(out=ident[:, :], in_=ident[:, :], compare_op=ALU.not_equal, fill=1.0,
                               base=0, pattern=[[-1, P]], channel_multiplier=1).then_inc(consts, 1)
            pool.affine_select(out=maskb[:, :], in_=maskb[:, :], compare_op=ALU.is_ge, fill=MASKED,
                               base=0, pattern=[[-1, P]], channel_multiplier=1).then_inc(consts, 1)
            pool.wait_ge(consts, 4)
            pool.tensor_copy(identb[:, :], ident[:, :]).then_inc(consts, 1)
            pool.memset(ones[:, :], 1.0).then_inc(consts, 1)
            pool.memset(onesrow[:, :], 1.0).then_inc(consts, 1)
            pool.wait_ge(consts, 6)
            pool.tensor_copy(ones_r[:, :], ones[:, :]).then_inc(consts, 1)

            def lo(c0, i=0, n=2048):
                s = c0 % 2
                pool.wait_ge(w_hi, c0 + 1 + 2 * i)
                pool.wait_ge(w_lo, c0 + RING + 2 * i)
                pool.tensor_tensor(wsplit[:, s, LO, 0:n], wraw[:, s, 0:n], wsplit[:, s, HI, 0:n].bitcast(FP32),
                                   ALU.subtract).then_inc(w_lo, 1)
            lo(C_RNN)
            lo(C_RNN + 1)

            with pool.Fori(0, NR // 2) as i:
                for t in range(2):
                    pool.wait_ge(sig_done, 4 * i + t + 1)
                    pool.wait_ge(conv_tap, 6 * i + 3 * t + 3)
                    pool.tensor_tensor(ig[:, t], ig[:, t], xc[:, t], ALU.mult).then_inc(ix_done, 1)
                for t in range(2):
                    pool.wait_ge(gelu_done, 2 * i + t + 1)
                    pool.wait_ge(scan_done, 2 * i + t + 1)
                    pool.tensor_tensor(gl[:, t], gl[:, t], th[:, t], ALU.mult).then_inc(y_done, 1)

            with pool.Fori(0, KD - 2) as j:
                lo(C_MIX + 3, j, KD * P)
            lo(C_UP + 1)

            def shift(b):
                for half in range(2 if b < NB - 1 else 1):
                    cs = slice(T * half, T * half + T)
                    pool.wait_ge(o_mul, 2 * b + half + 1)
                    pool.tensor_tensor(o_nat[:, b, cs], o_nat[:, b, cs], bc[:, 1, cs], ALU.add).then_inc(o_add, 1)
            for b in range(NB - 1):
                pool.wait_ge(x2_mul, 2 * b + 2)
                pool.tensor_tensor(x2[:, b, T:D], x2[:, b, T:D], x1_nat[:, b, T:D], ALU.add).then_inc(x2_add1, 1)
                if b:
                    shift(b - 1)
            shift(NB - 2)
            shift(NB - 1)

        @block.scalar
        def _(ae):
            def hi(c0, i=0, n=2048, stride=2):
                s = c0 % 2
                ae.wait_ge(w_loaded[s], landed(c0, i, stride))
                ae.wait_ge(w_used, c0 + 1 + stride * i)
                ae.activation(wsplit[:, s, HI, 0:n], wraw[:, s, 0:n], ACT.Copy).then_inc(w_hi, 1)

            def rows(a, r0, src, n):
                ae.dma_start(vrows[r0:r0 + n, a], src).then_inc(vec_loaded if a else vec_a_loaded, 16)

            def as_rows(v):
                return v.rearrange("(r p) -> r p", p=P)
            rows(0, V_BADA, as_rows(b_ada[0])[0:5 * KD], 5 * KD)
            rows(0, V_G1, as_rows(g_norm1[0]), KD)
            rows(0, V_CW, w_rnn_conv[0].rearrange("t (r p) -> (t r) p", p=P), 4 * NR)
            ae.wait_ge(c_loaded, 16)
            ae.activation(csig, ccol, ACT.Sigmoid).then_inc(csig_done, 1)
            rows(1, V_CB - V_ROWS_A, as_rows(b_rnn_conv[0]), NR)
            rows(1, V_BA - V_ROWS_A, as_rows(b_lru_a[0]), NR)
            rows(1, V_BI - V_ROWS_A, as_rows(b_lru_i[0]), NR)
            rows(1, V_LAM - V_ROWS_A, as_rows(lru_lambda[0]), NR)
            rows(1, V_G2 - V_ROWS_A, as_rows(g_norm2[0]), KD)
            rows(2, V_FW - V_ROWS_B, w_ffn_conv[0].rearrange("t (r p) -> (t r) p", p=P), 3 * NF)
            rows(2, V_FB - V_ROWS_B, as_rows(b_ffn_conv[0]), NF)
            ae.dma_start(fw[:, :, :], w_in_v[:, :, COL_FL:COL_FL + H]).then_inc(small_loaded, 16)
            ae.dma_start(bfg[:, :], b_fgate[0].rearrange("(h a) -> h a", a=1)).then_inc(small_loaded, 16)

            for b in range(NB):
                ae.wait_ge(x_loaded[b], 16)
                ae.activation(sq1[:, b], x_nat[:, b], ACT.Square, accum_out=ss1[:, b:b + 1])\
                  .then_inc(ms1_sum, 1)
            for k in range(KD):
                ae.wait_ge(xT_mm, k + 1)
                ae.activation(xT_out[:, k], ps[:, 2 + k % 4, :], ACT.Copy).then_inc(xT_copied, 1)
            ae.wait_ge(xT_copied, KD)
            ae.dma_start(xT_dram, xT_out[:, :, :]).then_inc(xT_stored, 16)
            ae.wait_ge(ms1_mean, 1)
            ae.activation(rs1, ss1, ACT.Sqrt).then_inc(ms1_sqrt, 1)
            ae.wait_ge(small_loaded, 32)
            ae.activation(fws[:, HI].rearrange("p k h -> p (k h)"),
                          fw[:, :, :].rearrange("p k h -> p (k h)"), ACT.Copy).then_inc(fw_hi, 1)
            hi(C_RNN)
            for k in range(KD):
                ae.wait_ge(h_tmp, k + 1)
                ae.activation(h[:, HI, k], htmp[:, k % 2], ACT.Identity,
                              bias=mod[:, M_SH1 + k:M_SH1 + k + 1]).then_inc(h_hi, 1)
                if k == 1:
                    hi(C_RNN + 1)
            ae.wait_ge(lam_step, 1)
            ae.activation(lam_e, lam_a, ACT.Exp).then_inc(lam_exp, 1)

            def conv_first(i, t):
                wait_from(ae, xr_part, 4 * i + 2 * t - 2)
                wait_from(ae, ix_done, 2 * i + t - 1)
                if t == 0:
                    ae.wait_ge(tile0, first(C_RNN, i))
                else:
                    ae.wait_ge(w_used, whole(C_RNN, i))
                ae.activation(xc[:, t], ps[:, t, :], ACT.Identity,
                              scale=vec[:, ds(V_CW + 3 * NR + t + 2 * i, 1)],
                              bias=vec[:, ds(V_CB + t + 2 * i, 1)]).then_inc(conv0, 1)

            def lru_high(i):
                ae.wait_ge(lru_loaded, 32 + 32 * i)
                wait_from(ae, gate_mm, 4 * i)
                ae.activation(lru_w[:, HI].rearrange("p a n d -> p (a n d)"),
                              lru_raw[:, :].rearrange("p a n d -> p (a n d)"), ACT.Copy)\
                  .then_inc(lru_hi, 1)

            def gates_first(i):
                ae.wait_ge(gate_mm, 4 * i + 4)
                wait_from(ae, scan_done, 2 * i)
                for t in range(2):
                    ae.activation(ig[:, t], ps[:, 6 + t, :], ACT.Sigmoid,
                                  bias=vec[:, ds(V_BI + t + 2 * i, 1)]).then_inc(sig_done, 1)
                for t in range(2):
                    ae.activation(rg[:, t], ps[:, 4 + t, :], ACT.Sigmoid,
                                  bias=vec[:, ds(V_BA + t + 2 * i, 1)]).then_inc(sig_done, 1)
                wait_from(ae, y_part, 4 * i)
                for t in range(2):
                    if t == 0:
                        ae.wait_ge(tile0, first(C_RNN + 1, i))
                    else:
                        ae.wait_ge(w_used, whole(C_RNN + 1, i))
                    ae.activation(gl[:, t], ps[:, 2 + t, :], ACT.Gelu_apprx_tanh).then_inc(gelu_done, 1)

            def gates_exp(i, pair=(0, 1)):
                ae.wait_ge(lam_step, LAM_STEPS)
                for t in pair:
                    ae.wait_ge(sig_done, 4 * i + 3 + t)
                    for dst, col, fn in ((av, sp_m8, ACT.Exp), (th, sp_p4, ACT.Tanh)):
                        ae.activation(dst[:, t], rg[:, t], fn, scale=col[:, ds(2 * i + t, 1)])\
                          .then_inc(exp_done, 1)

            def gates_sqrt(i):
                for t in range(2):
                    ae.wait_ge(q_done, 2 * i + t + 1)
                    ae.activation(ev[:, t], ev[:, t], ACT.Sqrt).then_inc(sqrt_done, 1)

            def rnn_step(i, inner=True):
                if inner:
                    hi(C_RNN + 1, i)
                lru_high(i)
                if inner:
                    gates_first(i - 1)
                conv_first(i, 0)
                if inner:
                    gates_exp(i - 1)
                conv_first(i, 1)
                hi(C_RNN + 2, i)
                if inner:
                    gates_sqrt(i - 1)

            ae.wait_ge(h_lo, KD)
            rnn_step(0, inner=False)
            with ae.Fori(1, NR // 2) as i:
                rnn_step(i)

            def branch_gate(j, c0, i=0):
                ae.wait_ge(w_used, whole(c0, i))
                ae.activation(merged_a[:, j], ps[:, 0 if c0 != C_MIX + 1 else 1, :], ACT.Sigmoid)\
                  .then_inc(sigr_done, 1)
            i = NR // 2 - 1
            hi(C_MIX + 1, 0, KD * P)
            gates_first(i)
            gates_exp(i, (0,))
            hi(C_MIX + 2, 0, NR * P)
            gates_exp(i, (1,))
            gates_sqrt(i)
            ae.wait_ge(ix_done, NR)
            branch_gate(0, C_MIX)
            branch_gate(1, C_MIX + 1)
            with ae.Fori(0, KD - 2) as j:
                hi(C_MIX + 3, j, KD * P)
                hi(C_MIX + 4, j, NR * P)
                branch_gate(j + 2, C_MIX + 3, j)
            hi(C_MIX + 15, 0, NR * P)
            ae.wait_ge(fl_step, 2)
            ae.activation(fl2[:, :], fl2[:, :], ACT.Exp).then_inc(fl_act, 1)
            ae.wait_ge(fl_step, 3)
            ae.activation(fl2[:, :], fl2[:, :], ACT.Ln).then_inc(fl_act, 1)
            hi(C_ATT)

            def qk_hi(i, t, which):
                c0 = C_ATT + which
                if t == 0:
                    ae.wait_ge(tile0, first(c0, i, 4))
                else:
                    ae.wait_ge(w_used, whole(c0, i, 4))
                ae.activation(qk[:, t, which, HI], ps[:, t, :], ACT.Copy,
                              scale=SCALE if which == 0 else 1.0).then_inc(att_hi, 1)

            def v_hi(i, half):
                if half == 0:
                    ae.wait_ge(tile0, first(C_ATT + 2, i, 4))
                else:
                    ae.wait_ge(w_used, whole(C_ATT + 2, i, 4))
                ae.activation(vh[:, HI, 2 * half:2 * half + 2].rearrange("p b d -> p (b d)"),
                              ps[:, half, :], ACT.Copy).then_inc(att_hi, 1)

            def gate_a(i, t):
                if t == 0:
                    ae.wait_ge(tile0, first(C_ATT - 1, i, 4))
                else:
                    ae.wait_ge(w_used, whole(C_ATT - 1, i, 4))
                ae.activation(sig_a[:, 2 * (i - 1) + t], ps[:, t, :], ACT.Sigmoid).then_inc(siga_done, 1)

            def exps(i, t):
                for turn, qb in enumerate(S_ORDER):
                    pr = prob[:, t, P_AT[qb]:P_AT[qb] + P * (qb + 1)]
                    ae.wait_ge(s_max, 8 * (i - 1) + 4 * t + turn + 1)
                    ae.activation(pr, pr, ACT.Exp, bias=nmx[:, t, qb:qb + 1],
                                  accum_out=psum_row[:, t, qb:qb + 1]).then_inc(p_exp, 1)

            def probs_hi(i, t):
                for g, (bank, a, n, to) in enumerate(PT_EVAC):
                    ae.wait_ge(t_mm, 6 * (i - 1) + 3 * t + g + 1)
                    ae.activation(pt[:, HI, to:to + n], ps[:, bank, a:a + n], ACT.Copy).then_inc(pt_hi, 1)

            def y_hi(i, t):
                ae.wait_ge(pv_mm, 2 * (i - 1) + t + 1)
                ae.activation(yatt[:, HI, 2 * (i - 1) + t], ps[:, 7, :], ACT.Copy).then_inc(ya_hi, 1)

            def att_step(i):
                hi(C_ATT, i, stride=4)
                exps(i, 0)
                gate_a(i, 0)
                exps(i, 1)
                gate_a(i, 1)
                probs_hi(i, 0)
                hi(C_ATT + 1, i, stride=4)
                qk_hi(i, 0, 0)
                y_hi(i, 0)
                probs_hi(i, 1)
                qk_hi(i, 1, 0)
                hi(C_ATT + 2, i, stride=4)
                y_hi(i, 1)
                qk_hi(i, 0, 1)
                qk_hi(i, 1, 1)
                hi(C_ATT + 3, i, stride=4)
                v_hi(i, 0)
                v_hi(i, 1)

            hi(C_ATT + 1)
            qk_hi(0, 0, 0)
            qk_hi(0, 1, 0)
            hi(C_ATT + 2)
            qk_hi(0, 0, 1)
            qk_hi(0, 1, 1)
            hi(C_ATT + 3)
            v_hi(0, 0)
            v_hi(0, 1)
            with ae.Fori(1, H // 2) as i:
                att_step(i)
            last = H // 2
            hi(C_PRA)
            exps(last, 0)
            gate_a(last, 0)
            exps(last, 1)
            gate_a(last, 1)
            probs_hi(last, 0)
            hi(C_PRA + 1)
            y_hi(last, 0)
            probs_hi(last, 1)
            y_hi(last, 1)

            for cc in range(4):
                if cc:
                    hi(C_PRA + 1 + cc)
                for t in range(2):
                    jt = 2 * cc + t
                    ae.wait_ge(mb_add, jt + 1)
                    ae.activation(h[:, HI, jt], mt[:, t], ACT.Copy).then_inc(mb_hi, 1)

            def x1_rows(half):
                for b in range(NB):
                    ae.wait_ge(x1n_mm, 4 * half + b + 1)
                    ae.activation(x1_nat[:, b, T * half:T * half + T], ps[:, 4 + b, :], ACT.Copy)\
                      .then_inc(x1n_done, 1)
            for cc in range(4):
                hi(C_OUT + 1 + cc)
                for t in range(2):
                    jt = 2 * cc + t
                    wait_from(ae, sq_added, jt - 1)
                    ae.wait_ge(x1_done, jt + 1)
                    ae.activation(sq2[:, t], x1T[:, jt], ACT.Square).then_inc(sq_done, 1)
                if cc == 2:
                    x1_rows(0)
            ae.wait_ge(ms2_mean, 1)
            ae.activation(rs2, ss2, ACT.Sqrt).then_inc(ms2_sqrt, 1)
            hi(C_UP + 1)
            for k in range(KD):
                ae.wait_ge(h2_tmp, k + 1)
                ae.activation(h[:, HI, k], htmp2[:, k % 2], ACT.Identity,
                              bias=mod[:, M_SH2 + k:M_SH2 + k + 1]).then_inc(h2_hi, 1)
            x1_rows(1)
            ae.wait_ge(h2_lo, KD)
            for dst, src in ((bc[:, 0], b_ada[:, 5 * D:6 * D]),
                             (bc[:, 1:3].rearrange("p v d -> p (v d)"),
                              b_ada_final.rearrange("(a n) -> a n", a=1)),
                             (g_rows[:, :], g_final.rearrange("(a n) -> a n", a=1))):
                ae.dma_start(dst, src.broadcast_to([P, src.shape[1]])).then_inc(bc_loaded, 16)

            def down_hi(c0, i=0):
                hi(c0, i)
                for u in range(2):
                    n = 2 * (c0 - C_DOWN) + u
                    ae.wait_ge(act_done, n + 1 + 4 * i)
                    ae.activation(act_s[:, 2 * (c0 % 2) + u, HI], act[:, n + 4 * i], ACT.Copy)\
                      .then_inc(act_hi, 1)

            def up_step(i, following, weights=True):
                if weights:
                    hi(C_UP + 1, i)
                for t in range(2):
                    if t == 0:
                        ae.wait_ge(tile0, first(C_UP, i))
                    else:
                        ae.wait_ge(w_used, whole(C_UP, i))
                    wait_from(ae, fgelu, 2 * i + t - 1)
                    ae.activation(cv[:, t], ps[:, t, :], ACT.Identity,
                                  scale=vec[:, ds(V_FW + 2 * NF + t + 2 * i, 1)],
                                  bias=vec[:, ds(V_FB + t + 2 * i, 1)]).then_inc(fconv0, 1)
                following(i)
                for t in range(2):
                    wait_from(ae, act_done, 2 * i + t - 1)
                    ae.wait_ge(fconv_tap, 4 * i + 2 * t + 2)
                    ae.activation(gg[:, t], cv[:, t], ACT.Gelu_apprx_tanh).then_inc(fgelu, 1)

            up_step(0, lambda i: hi(C_UP + 2, i), weights=False)
            with ae.Fori(1, NF // 2 - 1) as i:
                up_step(i, lambda i: hi(C_UP + 2, i))
            up_step(NF // 2 - 1, lambda i: down_hi(C_DOWN))
            with ae.Fori(0, NF // 4 - 1) as i:
                down_hi(C_DOWN + 1, i)
                down_hi(C_DOWN + 2, i)
            down_hi(C_END - 1)
            for b in range(NB):
                for half in range(2):
                    n = 2 * b + half
                    if half == 0:
                        ae.wait_ge(x2_add, b + 1)
                    elif b < NB - 1:
                        ae.wait_ge(x2_add1, b + 1)
                    else:
                        ae.wait_ge(x2_last, 1)
                    ae.activation(sqe[:, b, half], x2[:, b, T * half:T * half + T], ACT.Square,
                                  accum_out=ss3[:, n:n + 1]).then_inc(ms3_sum, 1)
                ae.wait_ge(ms3_mean, 2 * b + 2)
                ae.activation(rs3[:, b:b + 1], ms3[:, b:b + 1], ACT.Sqrt).then_inc(ms3_sqrt, 1)

        @block.vector
        def _(ve):
            F = FP32

            def lo(c0, i=0, n=2048, stride=2):
                s = c0 % 2
                ve.wait_ge(w_hi, c0 + 1 + stride * i)
                ve.tensor_tensor(wsplit[:, s, LO, 0:n], wraw[:, s, 0:n],
                                 wsplit[:, s, HI, 0:n].bitcast(F), ALU.subtract).then_inc(w_lo, 1)

            def ada_sums(acc, blocks, before):
                for n, (k, wait, w) in enumerate(blocks):
                    if wait:
                        ve.wait_ge(*wait)
                    if n == 0:
                        ve.tensor_scalar(acc, w, cact[:, k:k + 1], None, ALU.mult).then_inc(ada_part, 1)
                    else:
                        ve.wait_ge(ada_part, before + n)
                        ve.scalar_tensor_tensor(acc, w, cact[:, k:k + 1], acc, ALU.mult, ALU.add)\
                          .then_inc(ada_part, 1)

            def ada(idx):
                before = 8 * (idx - N_START) + ADA_FIRST
                ada_sums(ada_acc[:, :], [(k, (ada_loaded[k // 4], 16 * (idx - N_START) + 16) if k % 4 == 0 else None,
                                          ada_raw[:, k // 4, k % 4]) for k in range(KD)], before)
                ve.wait_ge(ada_mm, idx)
                ve.wait_ge(ada_part, before + 8)
                ve.tensor_copy(ada_split[:, HI], ada_acc[:, :]).then_inc(ada_hl, 1)
                ve.wait_ge(ada_hl, 2 * (idx - N_START) + 1)
                ve.tensor_tensor(ada_split[:, LO], ada_acc[:, :], ada_split[:, HI].bitcast(F), ALU.subtract)\
                  .then_inc(ada_hl, 1)

            def ada_first_sums(acc, quarters, before):
                ada_sums(acc, [(4 * (q % 2) + k, (ada_first_loaded[q], 16) if k == 0 else None, ada_first[:, q % 6, k])
                               for q in quarters for k in range(4)], before)

            def ada_store(idx, bank=6):
                ve.wait_ge(ada_mm, idx + 1)
                ve.tensor_tensor(ada_diag[:, :].rearrange("p (j n) -> p j n", j=4),
                                 ps[:, bank, :].rearrange("p (j n) -> p j n", j=4),
                                 ident[:, :].rearrange("p (a n) -> p a n", a=1).broadcast_to([P, 4, P]),
                                 ALU.mult).then_inc(ada_pick, 1)
                ve.wait_ge(ada_pick, idx + 1)
                m = mod[:, ds(4 * idx, 4)]
                ve.tensor_reduce(m, ada_diag[:, :].rearrange("p (j n) -> p j n", j=4), AX_X, ALU.add)\
                  .then_inc(ada_sum, 1)
                ve.wait_ge(ada_sum, idx + 1)
                ve.tensor_tensor(m, m, vec[:, ds(V_BADA + 4 * idx, 4)], ALU.add).then_inc(ada_out, 1)

            def ada_store_row(idx):
                ve.wait_ge(ada_mm, idx + 1)
                row = bc[:, :, :].rearrange("p v d -> p (v d)")[:, ds(T * idx - T * N_COLS, T)]
                ve.tensor_tensor(row, ps[:, 6, :], row, ALU.add).then_inc(ada_out, 1)

            newton_n = 0

            def newton(r, m):
                nonlocal newton_n
                t = newton_t[:, 0:r.shape[1]]
                for step in (lambda: ve.scalar_tensor_tensor(t, r, -0.5, r, ALU.mult, ALU.mult),
                             lambda: ve.tensor_tensor(t, t, m, ALU.mult),
                             lambda: ve.scalar_tensor_tensor(r, t, 1.5, r, ALU.add, ALU.mult)):
                    step().then_inc(newton_step, 1)
                    newton_n += 1
                    ve.wait_ge(newton_step, newton_n)

            ve.sem_inc(w_lo, RING)
            ve.sem_inc(lru_lo, 1)
            ve.wait_ge(csig_done, 1)
            ve.tensor_tensor(cact, ccol, csig, ALU.mult).then_inc(cact_done, 1)
            ve.wait_ge(cact_done, 1)
            ve.wait_ge(consts, 6)
            for k in range(KD):
                ve.tensor_scalar(cact_rows[:, k], ones[:, :], cact[:, k:k + 1], None, ALU.mult)\
                  .then_inc(cact_row, 1)
            ve.wait_ge(vec_mm, 1)
            ve.tensor_copy(vec[:, 0:V_ROWS_A], ps[:, 0, 0:V_ROWS_A]).then_inc(vec_ok, 1)
            ve.wait_ge(vec_ok, 1)
            ada_store(0)
            ve.wait_ge(ms1_sum, NB)
            ve.tensor_scalar(ss1, ss1, 1.0 / D, EPS, ALU.mult, ALU.add).then_inc(ms1_mean, 1)
            ve.wait_ge(ms1_sqrt, 1)
            ve.reciprocal(rs1, rs1).then_inc(rs1_done, 1)
            ve.wait_ge(rs1_done, 1)
            newton(rs1, ss1)
            for b in range(NB):
                ve.tensor_scalar(diag1[:, P * b:P * b + P], ident[:, :], rs1[:, b:b + 1], None, ALU.mult)\
                  .then_inc(diag1_done, 1)
            ada_first_sums(ada_acc[:, :], (4, 5), 0)
            ada_store(1, 1)
            ve.wait_ge(vec_mm, 2)
            ve.tensor_copy(vec[:, V_ROWS_A:V_END], ps[:, 0, V_ROWS_A:V_END]).then_inc(vec_ok, 1)
            ve.wait_ge(vec_ok, 2)
            lam = vec[:, V_LAM:V_LAM + NR]
            ve.scalar_tensor_tensor(lam_a, lam, -1.0, lam, ALU.mult, ALU.min).then_inc(lam_step, 1)
            ada_first_sums(htmp[:, 0], (7,), 8)
            ada_store(2, 5)
            ve.wait_ge(fw_hi, 1)
            ve.tensor_tensor(fws[:, LO].rearrange("p k h -> p (k h)"), fw[:, :, :].rearrange("p k h -> p (k h)"),
                             fws[:, HI].rearrange("p k h -> p (k h)").bitcast(F), ALU.subtract).then_inc(fw_lo, 1)
            ada_store(3)
            ve.wait_ge(ada_out, 4)
            ve.scalar_tensor_tensor(gs1, mod[:, M_SC1:M_SC1 + KD], 1.0, vec[:, V_G1:V_G1 + KD],
                                    ALU.add, ALU.mult).then_inc(gs_done, 1)
            ve.wait_ge(gs_done, 1)
            ve.wait_ge(rs1_mm, 1)
            ve.wait_ge(xT_copied, KD)

            def h_low(k):
                ve.wait_ge(h_hi, k + 1)
                ve.scalar_tensor_tensor(h[:, LO, k], htmp[:, k % 2], mod[:, M_SH1 + k:M_SH1 + k + 1],
                                        h[:, HI, k].bitcast(F), ALU.add, ALU.subtract).then_inc(h_lo, 1)
            for k in range(KD):
                wait_from(ve, h_lo, k - 1)
                ve.scalar_tensor_tensor(htmp[:, k % 2], xT_out[:, k], gs1[:, k:k + 1], ps[:, 7, :],
                                        ALU.mult, ALU.mult).then_inc(h_tmp, 1)
                if k:
                    h_low(k - 1)
            h_low(KD - 1)

            def conv(i, t):
                ve.wait_ge(conv0, 2 * i + t + 1)
                for d in range(1, 4):
                    if d > 1:
                        ve.wait_ge(conv_tap, 6 * i + 3 * t + d - 1)
                    ve.scalar_tensor_tensor(xc[:, t, d:T], ps[:, t, 0:T - d],
                                            vec[:, ds(V_CW + (3 - d) * NR + t + 2 * i, 1)], xc[:, t, d:T],
                                            ALU.mult, ALU.add).then_inc(conv_tap, 1)

            def xr_split(i, t):
                wait_from(ve, gate_mm, 4 * i)
                ve.wait_ge(conv_tap, 6 * i + 3 * t + 3)
                ve.tensor_copy(xrs[:, t, HI], xc[:, t]).then_inc(xr_part, 1)
                ve.wait_ge(xr_part, 4 * i + 2 * t + 1)
                ve.tensor_tensor(xrs[:, t, LO], xc[:, t], xrs[:, t, HI].bitcast(F), ALU.subtract)\
                  .then_inc(xr_part, 1)

            def lru_low(i):
                ve.wait_ge(lru_hi, 1 + i)
                ve.tensor_tensor(lru_w[:, LO].rearrange("p a n d -> p (a n d)"),
                                 lru_raw[:, :].rearrange("p a n d -> p (a n d)"),
                                 lru_w[:, HI].rearrange("p a n d -> p (a n d)").bitcast(F), ALU.subtract)\
                  .then_inc(lru_lo, 1)

            def decay(i, pair=(0, 1)):
                for t in pair:
                    ve.wait_ge(exp_done, 4 * i + 2 * t + 2)
                    ve.scalar_tensor_tensor(ev[:, t], av[:, t], 1.0, th[:, t], ALU.add, ALU.mult)\
                      .then_inc(na_done, 1)
                for t in pair:
                    ve.wait_ge(na_done, 2 * i + t + 1)
                    ve.tensor_scalar(av[:, t], ev[:, t], -1.0, 1.0, ALU.mult, ALU.add).then_inc(a_done, 1)
                for t in pair:
                    ve.wait_ge(a_done, 2 * i + t + 1)
                    ve.scalar_tensor_tensor(ev[:, t], av[:, t], 1.0, ev[:, t], ALU.add, ALU.mult)\
                      .then_inc(q_done, 1)

            def recur(i, t):
                ve.wait_ge(sqrt_done, 2 * i + t + 1)
                ve.wait_ge(ix_done, 2 * i + t + 1)
                ve.tensor_tensor(ig[:, t], ev[:, t], ig[:, t], ALU.mult).then_inc(u_done, 1)
                ve.wait_ge(u_done, 2 * i + t + 1)
                ve.tensor_tensor_scan(th[:, t], av[:, t], ig[:, t], 0.0, ALU.mult, ALU.add)\
                  .then_inc(scan_done, 1)

            def y_split(i, t):
                ve.wait_ge(y_done, 2 * i + t + 1)
                ve.tensor_copy(yrnn[:, HI, 2 * i + t], gl[:, t]).then_inc(y_part, 1)
                ve.wait_ge(y_part, 4 * i + 2 * t + 1)
                ve.tensor_tensor(yrnn[:, LO, 2 * i + t], gl[:, t], yrnn[:, HI, 2 * i + t].bitcast(F),
                                 ALU.subtract).then_inc(y_part, 1)

            def rnn_step(i, inner=True):
                if inner:
                    lo(C_RNN + 1, i)
                lru_low(i)
                conv(i, 0)
                xr_split(i, 0)
                if inner:
                    decay(i - 1)
                conv(i, 1)
                xr_split(i, 1)
                lo(C_RNN + 2, i)
                if inner:
                    recur(i - 1, 0)
                    recur(i - 1, 1)
                    y_split(i - 1, 0)
                    y_split(i - 1, 1)

            ve.wait_ge(w_lo, RING + 2)
            rnn_step(0, inner=False)
            n = 1

            def lam_do(ins):
                nonlocal n
                ins.then_inc(lam_step, 1)
                n += 1
                ve.wait_ge(lam_step, n)
            ve.wait_ge(lam_exp, 1)
            lam_do(ve.tensor_scalar(lam_t, lam_e, 2.0, None, ALU.add))
            lam_do(ve.reciprocal(lam_t, lam_t))
            lam_do(ve.tensor_tensor(lam_t, lam_t, lam_e, ALU.mult))
            lam_do(ve.tensor_tensor(lam_u, lam_t, lam_t, ALU.mult))
            lam_do(ve.tensor_scalar(lam_p, lam_u, 2.0 / 17, 2.0 / 15, ALU.mult, ALU.add))
            for d in (13, 11, 9, 7, 5, 3, 1):
                lam_do(ve.tensor_tensor(lam_p, lam_p, lam_u, ALU.mult))
                lam_do(ve.tensor_scalar(lam_p, lam_p, 2.0 / d, None, ALU.add))
            lam_do(ve.tensor_tensor(lam_p, lam_p, lam_t, ALU.mult))
            lam_do(ve.tensor_scalar(lam_u, lam, -1.0, 0.0, ALU.mult, ALU.max))
            lam_do(ve.tensor_tensor(lam_p, lam_p, lam_u, ALU.add))
            lam_do(ve.tensor_scalar(sp_m8, lam_p, -LRU_C, None, ALU.mult))
            lam_do(ve.tensor_scalar(sp_p4, lam_p, LRU_C / 2, None, ALU.mult))
            assert n == LAM_STEPS
            ve.wait_ge(xT_stored, 16)
            ve.wait_ge(h_tmp, KD)
            with ve.Fori(1, NR // 2) as i:
                rnn_step(i)

            i = NR // 2 - 1
            lo(C_MIX + 1, 0, KD * P)
            decay(i, (0,))
            lo(C_MIX + 2, 0, NR * P)
            decay(i, (1,))
            recur(i, 0)
            recur(i, 1)
            y_split(i, 0)
            y_split(i, 1)
            def gate_product(j, c0, i=0):
                ve.wait_ge(sigr_done, j + 1)
                ve.wait_ge(w_used, whole(c0, i))
                ve.tensor_tensor(merged_a[:, j], ps[:, 2 if c0 != C_MIX + 15 else 1, :], merged_a[:, j], ALU.mult)\
                  .then_inc(mixa_done, 1)
            with ve.Fori(0, KD - 2) as j:
                ada(4 + j)
                gate_product(j, C_MIX + 2, j)
                ve.wait_ge(w_lo, whole(C_MIX + 3, j))
                lo(C_MIX + 4, j, NR * P)
                ada_store(4 + j)
            lo(C_MIX + 15, 0, NR * P)
            ve.wait_ge(fl_mm, 1)
            ve.wait_ge(small_loaded, 32)
            ve.wait_ge(consts, 7)
            ve.tensor_scalar(fl1[:, :], ps[0:H, 3, :], bfg[:, 0:1], None, ALU.add).then_inc(fl_step, 1)
            ve.wait_ge(fl_step, 1)
            ve.scalar_tensor_tensor(fl2[:, :], fl1[:, :], -1.0, fl1[:, :], ALU.mult, ALU.min).then_inc(fl_step, 1)
            ve.wait_ge(fl_act, 1)
            ve.tensor_scalar(fl2[:, :], fl2[:, :], 1.0, None, ALU.add).then_inc(fl_step, 1)
            ve.tensor_scalar(fl1[:, :], fl1[:, :], 0.0, None, ALU.min).then_inc(fl_step, 1)
            ve.wait_ge(fl_act, 2)
            ve.wait_ge(fl_step, 4)
            ve.tensor_tensor(fl1[:, :], fl2[:, :], fl1[:, :], ALU.subtract).then_inc(fl_step, 1)
            ve.wait_ge(fl_step, 5)
            ve.tensor_tensor_scan(nF[:, :], onesrow[:, :], fl1[:, :], 0.0, ALU.mult, ALU.add)\
              .then_inc(fl_step, 1)
            gate_product(KD - 2, C_MIX + 14)
            lo(C_ATT)
            gate_product(KD - 1, C_MIX + 15)
            ve.wait_ge(nFq_mm, 1)
            ve.tensor_copy(nFq[:, :, :].rearrange("p b h -> p (b h)"), ps[:, 3, 0:NB * H]).then_inc(fl_step, 1)
            ve.wait_ge(fl_step, 7)

            def qk_lo(i, t, which):
                n0 = 1 + 2 * which + t
                ve.wait_ge(att_hi, n0 + 6 * i)
                ve.scalar_tensor_tensor(qk[:, t, which, LO], ps[:, t, :], SCALE if which == 0 else 1.0,
                                        qk[:, t, which, HI].bitcast(F), ALU.mult, ALU.subtract)\
                  .then_inc(att_lo, 1)

            def v_lo(i, half):
                ve.wait_ge(att_hi, 5 + half + 6 * i)
                sl = slice(2 * half, 2 * half + 2)
                ve.tensor_tensor(vh[:, LO, sl].rearrange("p b d -> p (b d)"), ps[:, half, :],
                                 vh[:, HI, sl].rearrange("p b d -> p (b d)").bitcast(F), ALU.subtract)\
                  .then_inc(att_lo, 1)

            def scores_add(i, t):
                if t == 0:
                    ve.wait_ge(nF_loaded, 16 * i)
                for turn, qb in enumerate(S_ORDER):
                    n = P * (qb + 1)
                    bank, a = S_AT[qb]
                    pr = prob[:, t, P_AT[qb]:P_AT[qb] + n]
                    ve.wait_ge(s_mm, 8 * (i - 1) + 4 * t + S_READY[turn])
                    ve.scalar_tensor_tensor(pr, ps[:, bank, a:a + n], nFq[:, qb, ds(2 * (i - 1) + t, 1)],
                                            nFb[:, t, 0:n], ALU.subtract, ALU.add).then_inc(s_add, 1)
                    ve.wait_ge(s_add, 8 * (i - 1) + 4 * t + turn + 1)
                    ve.tensor_reduce(nmx[:, t, qb:qb + 1], pr, AX_X, ALU.max, negate=True).then_inc(s_max, 1)

            def probs_norm(i, t):
                ve.wait_ge(p_exp, 8 * (i - 1) + 4 * t + 4)
                ve.reciprocal(rsum[:, t], psum_row[:, t]).then_inc(p_rec, 1)
                ve.wait_ge(p_rec, 2 * (i - 1) + t + 1)
                for qb in range(NB):
                    pr = prob[:, t, P_AT[qb]:P_AT[qb] + P * (qb + 1)]
                    ve.tensor_scalar(pr, pr, rsum[:, t, qb:qb + 1], None, ALU.mult).then_inc(p_norm, 1)

            def probs_lo(i, t):
                for g, (bank, a, n, to) in enumerate(PT_EVAC):
                    ve.wait_ge(pt_hi, 6 * (i - 1) + 3 * t + g + 1)
                    ve.tensor_tensor(pt[:, LO, to:to + n], ps[:, bank, a:a + n],
                                     pt[:, HI, to:to + n].bitcast(F), ALU.subtract).then_inc(pt_lo, 1)

            def y_lo(i, t):
                ve.wait_ge(ya_hi, 2 * (i - 1) + t + 1)
                ve.tensor_tensor(yatt[:, LO, 2 * (i - 1) + t], ps[:, 7, :],
                                 yatt[:, HI, 2 * (i - 1) + t].bitcast(F), ALU.subtract).then_inc(ya_lo, 1)

            def att_step(i):
                scores_add(i, 0)
                lo(C_ATT, i, stride=4)
                probs_norm(i, 0)
                scores_add(i, 1)
                probs_norm(i, 1)
                probs_lo(i, 0)
                lo(C_ATT + 1, i, stride=4)
                qk_lo(i, 0, 0)
                y_lo(i, 0)
                probs_lo(i, 1)
                qk_lo(i, 1, 0)
                lo(C_ATT + 2, i, stride=4)
                y_lo(i, 1)
                qk_lo(i, 0, 1)
                qk_lo(i, 1, 1)
                lo(C_ATT + 3, i, stride=4)
                v_lo(i, 0)
                v_lo(i, 1)

            lo(C_ATT + 1)
            qk_lo(0, 0, 0)
            qk_lo(0, 1, 0)
            lo(C_ATT + 2)
            qk_lo(0, 0, 1)
            qk_lo(0, 1, 1)
            lo(C_ATT + 3)
            v_lo(0, 0)
            v_lo(0, 1)
            with ve.Fori(1, H // 2) as i:
                att_step(i)
            last = H // 2
            scores_add(last, 0)
            lo(C_PRA)
            probs_norm(last, 0)
            scores_add(last, 1)
            probs_norm(last, 1)
            probs_lo(last, 0)
            lo(C_PRA + 1)
            y_lo(last, 0)
            probs_lo(last, 1)
            y_lo(last, 1)

            for cc in range(4):
                if cc:
                    lo(C_PRA + 1 + cc)
                for t in range(2):
                    jt = 2 * cc + t
                    wait_from(ve, mb_lo, jt - 1)
                    if t == 0:
                        ve.wait_ge(tile0, first(C_PRA + cc))
                    else:
                        ve.wait_ge(w_used, whole(C_PRA + cc))
                    ve.wait_ge(siga_done, jt + 1)
                    ve.tensor_tensor(mt[:, t], ps[:, 2 * (cc % 2) + t, :], sig_a[:, jt], ALU.mult)\
                      .then_inc(mb_mul, 1)
                    ve.wait_ge(mb_mul, jt + 1)
                    ve.tensor_tensor(mt[:, t], mt[:, t], merged_a[:, jt], ALU.add).then_inc(mb_add, 1)
                for t in range(2):
                    jt = 2 * cc + t
                    ve.wait_ge(mb_hi, jt + 1)
                    ve.tensor_tensor(h[:, LO, jt], mt[:, t], h[:, HI, jt].bitcast(F), ALU.subtract)\
                      .then_inc(mb_lo, 1)
            ve.wait_ge(ada_out, 10)
            ve.scalar_tensor_tensor(gs2, mod[:, M_SC2:M_SC2 + KD], 1.0, vec[:, V_G2:V_G2 + KD],
                                    ALU.add, ALU.mult).then_inc(gs_done, 1)

            ve.wait_ge(xT_loaded, 16)
            for cc in range(4):
                lo(C_OUT + 1 + cc)
                for t in range(2):
                    jt = 2 * cc + t
                    if t == 0:
                        ve.wait_ge(tile0, first(C_OUT + cc))
                    else:
                        ve.wait_ge(w_used, whole(C_OUT + cc))
                    ve.scalar_tensor_tensor(x1T[:, jt], ps[:, 2 * (cc % 2) + t, :],
                                            mod[:, M_GT1 + jt:M_GT1 + jt + 1], x1T[:, jt],
                                            ALU.mult, ALU.add).then_inc(x1_done, 1)
                for t in range(2):
                    jt = 2 * cc + t
                    ve.wait_ge(sq_done, jt + 1)
                    if jt == 0:
                        ve.tensor_copy(sqacc[:, :], sq2[:, 0]).then_inc(sq_added, 1)
                    else:
                        ve.wait_ge(sq_added, jt)
                        ve.tensor_tensor(sqacc[:, :], sqacc[:, :], sq2[:, t], ALU.add).then_inc(sq_added, 1)

            ve.wait_ge(ms2_mm, 1)
            ve.tensor_scalar(ss2, ps[:, 2, 0:NB], 1.0 / D, EPS, ALU.mult, ALU.add).then_inc(ms2_mean, 1)
            ve.wait_ge(ms2_sqrt, 1)
            ve.reciprocal(rs2, rs2).then_inc(rs2_done, 1)
            ve.wait_ge(rs2_done, 1)
            newton(rs2, ss2)
            for b in range(NB):
                ve.tensor_scalar(diag[:, P * b:P * b + P], ident[:, :], rs2[:, b:b + 1], None, ALU.mult)\
                  .then_inc(diag_done, 1)
            ve.wait_ge(rs2_mm, 1)
            ve.wait_ge(gs_done, 2)

            def h2_low(k):
                ve.wait_ge(h2_hi, k + 1)
                ve.scalar_tensor_tensor(h[:, LO, k], htmp2[:, k % 2], mod[:, M_SH2 + k:M_SH2 + k + 1],
                                        h[:, HI, k].bitcast(F), ALU.add, ALU.subtract).then_inc(h2_lo, 1)
            for k in range(KD):
                wait_from(ve, h2_lo, k - 1)
                ve.scalar_tensor_tensor(htmp2[:, k % 2], x1T[:, k], gs2[:, k:k + 1], ps[:, 3, :],
                                        ALU.mult, ALU.mult).then_inc(h2_tmp, 1)
                if k:
                    h2_low(k - 1)
            h2_low(KD - 1)

            def down_lo(c0, i=0):
                lo(c0, i)
                for u in range(2):
                    n = 2 * (c0 - C_DOWN) + u
                    sl = 2 * (c0 % 2) + u
                    ve.wait_ge(act_hi, n + 1 + 4 * i)
                    ve.tensor_tensor(act_s[:, sl, LO], act[:, n + 4 * i], act_s[:, sl, HI].bitcast(F),
                                     ALU.subtract).then_inc(act_lo, 1)

            def up_step(i, following, idx=None, weights=True):
                if weights:
                    lo(C_UP + 1, i)
                for t in range(2):
                    if t == 1 and idx is not None:
                        ada(idx)
                    ve.wait_ge(fconv0, 2 * i + t + 1)
                    for d in range(1, 3):
                        if d > 1:
                            ve.wait_ge(fconv_tap, 4 * i + 2 * t + d - 1)
                        ve.scalar_tensor_tensor(cv[:, t, d:T], ps[:, t, 0:T - d],
                                                vec[:, ds(V_FW + (2 - d) * NF + t + 2 * i, 1)],
                                                cv[:, t, d:T], ALU.mult, ALU.add).then_inc(fconv_tap, 1)
                following(i)
                for t in range(2):
                    ve.wait_ge(fgelu, 2 * i + t + 1)
                    if t == 0:
                        ve.wait_ge(tile0, first(C_UP + 1, i))
                    else:
                        ve.wait_ge(w_used, whole(C_UP + 1, i))
                    ve.tensor_tensor(act[:, 2 * i + t], gg[:, t], ps[:, 2 + t, :], ALU.mult)\
                      .then_inc(act_done, 1)
                if idx is not None:
                    ada_store_row(idx)

            ve.wait_ge(w_lo, C_UP + RING + 2)
            up_step(0, lambda i: lo(C_UP + 2, i), weights=False)
            ve.wait_ge(bc_loaded, 48)
            with ve.Fori(1, 7) as i:
                up_step(i, lambda i: lo(C_UP + 2, i), 9 + i)
            ve.wait_ge(ada_out, 16)
            ve.scalar_tensor_tensor(bc[:, 2], bc[:, 2], 1.0, g_rows[:, :], ALU.add, ALU.mult).then_inc(bc_done, 1)
            with ve.Fori(7, NF // 2 - 1) as i:
                up_step(i, lambda i: lo(C_UP + 2, i))
            up_step(NF // 2 - 1, lambda i: down_lo(C_DOWN))
            with ve.Fori(0, NF // 4 - 1) as i:
                down_lo(C_DOWN + 1, i)
                down_lo(C_DOWN + 2, i)
            down_lo(C_END - 1)

            def gate_y(b):
                for half in range(2):
                    n, cs = 2 * b + half, slice(T * half, T * half + T)
                    ve.wait_ge(down_mm, n + 1)
                    ve.tensor_tensor(x2[:, b, cs], ps[:, n, :], bc[:, 0, cs], ALU.mult).then_inc(x2_mul, 1)
                for half in range(2 if b == NB - 1 else 1):
                    n, cs = 2 * b + half, slice(T * half, T * half + T)
                    ve.wait_ge(x2_mul, n + 1)
                    ve.tensor_tensor(x2[:, b, cs], x2[:, b, cs], x1_nat[:, b, cs], ALU.add)\
                      .then_inc(x2_last if half else x2_add, 1)
            ve.wait_ge(bc_done, 1)
            gate_y(0)
            for b in range(NB):
                if b + 1 < NB:
                    gate_y(b + 1)
                ve.wait_ge(ms3_sum, 2 * b + 2)
                ve.tensor_tensor(ms3[:, b:b + 1], ss3[:, 2 * b:2 * b + 1], ss3[:, 2 * b + 1:2 * b + 2], ALU.add)\
                  .then_inc(ms3_mean, 1)
                ve.wait_ge(ms3_mean, 2 * b + 1)
                ve.tensor_scalar(ms3[:, b:b + 1], ms3[:, b:b + 1], 1.0 / D, EPS, ALU.mult, ALU.add)\
                  .then_inc(ms3_mean, 1)
                ve.wait_ge(ms3_sqrt, b + 1)
                ve.reciprocal(rs3[:, b:b + 1], rs3[:, b:b + 1]).then_inc(rs3_done, 1)
                ve.wait_ge(rs3_done, b + 1)
                newton(rs3[:, b:b + 1], ms3[:, b:b + 1])
                for half in range(2):
                    cs = slice(T * half, T * half + T)
                    ve.scalar_tensor_tensor(o_nat[:, b, cs], x2[:, b, cs], rs3[:, b:b + 1], bc[:, 2, cs],
                                            ALU.mult, ALU.mult).then_inc(o_mul, 1)
            ve.wait_ge(o_mul, 2 * NB)
            ve.tensor_tensor(o_nat[:, NB - 1, T:D], o_nat[:, NB - 1, T:D], bc[:, 1, T:D], ALU.add)\
              .then_inc(o_last, 1)

        @block.tensor
        def _(te):
            def mm3(dst, lhs, rhs, start, stop):
                te.matmul(dst, lhs(LO), rhs(HI), start=start, stop=False)
                te.matmul(dst, lhs(HI), rhs(LO), start=False, stop=False)
                return te.matmul(dst, lhs(HI), rhs(HI), start=False, stop=stop)

            def w_tile(s, k, t, n):
                return lambda part: wsplit[:, s, part, k * n + P * t:k * n + P * t + P]

            def features(x_, k):
                return lambda part: x_[:, part, k]

            def project(c0, x_, bank, t, n=256, kk=KD, ready=None):
                for k in range(kk):
                    if ready:
                        ready(k)
                    ins = mm3(ps[:, bank, :], w_tile(c0 % 2, k, t, n), features(x_, k), k == 0, k == kk - 1)
                return ins

            def project2(c0, x_, bank, ready):
                for k in range(KD):
                    ready(k)
                    for t in range(2):
                        ins = mm3(ps[:, bank + t, :], w_tile(c0 % 2, k, t, 256), features(x_, k),
                                  k == 0, k == KD - 1)
                        if k == KD - 1:
                            ins.then_inc(tile0 if t == 0 else w_used, 1)

            def ada_total(idx):
                te.wait_ge(ada_hl, 2 * (idx - N_START) + 2)
                te.wait_ge(ada_out, idx)
                te.matmul(ps[:, 6, :], ones_r[:, :], ada_split[:, LO], start=True, stop=False)
                te.matmul(ps[:, 6, :], ones_r[:, :], ada_split[:, HI], start=False, stop=True).then_inc(ada_mm, 1)

            def ada_whole(idx, bank, quarters=(0, 1)):
                for q in quarters:
                    te.wait_ge(ada_first_loaded[2 * idx + q], 16)
                    for k in range(4 * q, 4 * q + 4):
                        ins = te.matmul(ps[:, bank, :], cact_rows[:, k], ada_first[:, (2 * idx + q) % 6, k % 4],
                                        start=k == 0, stop=k == KD - 1)
                if quarters[-1] == 1:
                    ins.then_inc(ada_mm, 1)

            def keep_clock(n, bank=0):
                for _ in range(n):
                    te.matmul(ps[:, bank, 0:P], ones[:, :], ident[:, :], start=True, stop=True)

            te.sem_inc(w_used, RING)
            te.wait_ge(cact_row, KD)
            ada_whole(0, 6)
            te.wait_ge(vec_a_loaded, 16 * 3)
            te.transpose(ps[:, 0, 0:V_ROWS_A], vrows[0:V_ROWS_A, 0], ident[0:V_ROWS_A, 0:V_ROWS_A])\
              .then_inc(vec_mm, 1)
            for b in range(NB):
                te.wait_ge(x_loaded[b], 16)
            for k in range(KD):
                if k >= 4:
                    te.wait_ge(xT_copied, k - 3)
                for b in range(NB):
                    ins = te.transpose(ps[:, 2 + k % 4, P * b:P * b + P], x_nat[:, b, P * k:P * k + P],
                                       ident[:, :])
                ins.then_inc(xT_mm, 1)
            ada_whole(1, 1)
            te.wait_ge(diag1_done, NB)
            te.matmul(ps[:, 7, :], ones[:, :], diag1[:, :], start=True, stop=True).then_inc(rs1_mm, 1)
            te.wait_ge(vec_loaded, 16 * 7)
            te.wait_ge(vec_ok, 1)
            nb_, nc_ = V_ROWS_B - V_ROWS_A, V_END - V_ROWS_B
            te.transpose(ps[:, 0, V_ROWS_A:V_ROWS_B], vrows[0:nb_, 1], ident[0:nb_, 0:nb_])
            te.transpose(ps[:, 0, V_ROWS_B:V_END], vrows[0:nc_, 2], ident[0:nc_, 0:nc_]).then_inc(vec_mm, 1)
            te.wait_ge(xT_copied, KD)
            keep_clock(15, 2)
            te.wait_ge(ada_out, 1)
            ada_whole(3, 6, (0,))
            te.wait_ge(ada_part, 8)
            te.matmul(ps[:, 5, :], ones[:, :], ada_acc[:, :], start=True, stop=True).then_inc(ada_mm, 1)
            te.wait_ge(ada_part, ADA_FIRST)
            te.matmul(ps[:, 6, :], ones[:, :], htmp[:, 0], start=False, stop=True).then_inc(ada_mm, 1)
            te.wait_ge(consts, 8)
            te.wait_ge(vec_ok, 2)
            keep_clock(22)

            def rnn_gates(i):
                te.wait_ge(lru_lo, 2 + i)
                wait_from(te, sig_done, 4 * i)
                for t in range(2):
                    te.wait_ge(xr_part, 4 * i + 2 * t + 2)
                    for g in range(2):
                        mm3(ps[:, 4 + 2 * g + t, :], lambda part: lru_w[:, part, g, t],
                            lambda part: xrs[:, t, part], True, True).then_inc(gate_mm, 1)

            def rnn_step(i, peeled=False):
                te.wait_ge(w_lo, whole(C_RNN, i))
                if peeled:
                    project2(C_RNN, h, 0, lambda k: te.wait_ge(h_lo, k + 1))
                else:
                    te.wait_ge(conv_tap, 6 * i)
                    project(C_RNN, h, 0, 0).then_inc(tile0, 1)
                    project(C_RNN, h, 1, 1).then_inc(w_used, 1)
                te.wait_ge(w_lo, whole(C_RNN + 1, i))
                wait_from(te, gelu_done, 2 * i)
                project(C_RNN + 1, h, 2, 0).then_inc(tile0, 1)
                project(C_RNN + 1, h, 3, 1).then_inc(w_used, 1)
                rnn_gates(i)

            rnn_step(0, peeled=True)
            with te.Fori(1, NR // 2) as i:
                rnn_step(i)

            def gate_mr(c0, bank, i=0):
                te.wait_ge(w_lo, whole(c0, i))
                project(c0, h, bank, 0, P).then_inc(w_used, 1)

            def proj_rnn(c0, bank, i=0, y_ready=None):
                te.wait_ge(w_lo, whole(c0, i))
                project(c0, yrnn, bank, 0, P, NR, y_ready).then_inc(w_used, 1)

            te.wait_ge(conv_tap, 3 * NR)
            gate_mr(C_MIX, 0)
            gate_mr(C_MIX + 1, 1)
            te.wait_ge(gelu_done, NR)
            te.wait_ge(fw_lo, 1)
            for k in range(KD):
                ins = mm3(ps[0:H, 3, :], lambda part: fws[:, part, k], features(h, k), k == 0, k == KD - 1)
            ins.then_inc(fl_mm, 1)
            proj_rnn(C_MIX + 2, 2, 0, lambda k: te.wait_ge(y_part, 2 * k + 2))
            te.wait_ge(sigr_done, 2)
            gate_mr(C_MIX + 3, 0)
            ada_total(4)
            with te.Fori(1, KD - 2) as j:
                te.wait_ge(mixa_done, j)
                proj_rnn(C_MIX + 2, 2, j)
                te.wait_ge(sigr_done, j + 2)
                gate_mr(C_MIX + 3, 0, j)
                ada_total(4 + j)
            te.wait_ge(mixa_done, KD - 2)
            proj_rnn(C_MIX + 14, 2)
            proj_rnn(C_MIX + 15, 1)
            te.wait_ge(fl_step, 6)
            for b in range(NB):
                ins = te.transpose(ps[:, 3, H * b:H * b + H], nF[:, P * b:P * b + P], ident[0:H, 0:H])
            ins.then_inc(nFq_mm, 1)

            def qk_proj(i, which, t):
                c0 = C_ATT + which
                if t == 0:
                    te.wait_ge(w_lo, whole(c0, i, 4))
                project(c0, h, t, t).then_inc(tile0 if t == 0 else w_used, 1)

            def v_proj(i):
                te.wait_ge(w_lo, whole(C_ATT + 2, i, 4))
                s = C_ATT % 2
                for b in range(NB):
                    if b % 2 == 0:
                        te.wait_ge(att_lo, 3 + b // 2 + 6 * i)
                    for k in range(KD):
                        ins = mm3(ps[:, b // 2, 256 * (b % 2):256 * (b % 2) + 256],
                                  lambda part: h[:, part, k, P * b:P * b + P],
                                  lambda part: wsplit[:, s, part, 256 * k:256 * k + 256], k == 0, k == KD - 1)
                    if b == 1:
                        ins.then_inc(tile0, 1)
                ins.then_inc(w_used, 1)

            def gate_proj(i, t):
                if t == 0:
                    te.wait_ge(w_lo, whole(C_ATT - 1, i, 4))
                te.wait_ge(att_lo, 6 * (i - 1) + 5 + t)
                project(C_ATT - 1, h, t, t).then_inc(tile0 if t == 0 else w_used, 1)

            def scores(i, t):
                te.wait_ge(att_lo, 6 * (i - 1) + 4)
                if t == 1:
                    te.wait_ge(s_add, 8 * (i - 1) + 4)
                te.wait_ge(fl_step, 7)
                for qb in S_ORDER:
                    n = P * (qb + 1)
                    bank, a = S_AT[qb]
                    mm3(ps[:, bank, a:a + n], lambda part: qk[:, t, 0, part, P * qb:P * qb + P],
                        lambda part: qk[:, t, 1, part, 0:n], True, False)
                    te.matmul(ps[:, bank, a + n - P:a + n], identb[:, :], maskb[:, :], start=False, stop=True)\
                      .then_inc(s_mm, 1)

            def prob_transposes(i, t):
                te.wait_ge(p_norm, 8 * (i - 1) + 4 * t + 4)
                for kbs in ((0,), (1, 3), (2,)):
                    if kbs == (2,) and t == 0:
                        te.wait_ge(s_add, 8 * (i - 1) + 8)
                    for kb in kbs:
                        bank, a, _ = PT_AT[kb]
                        for qb in range(kb, NB):
                            at_ = a + P * (qb - kb)
                            pcol = P_AT[qb] + P * kb
                            ins = te.transpose(ps[:, bank, at_:at_ + P], prob[:, t, pcol:pcol + P], ident[:, :])
                    ins.then_inc(t_mm, 1)

            def weighted(i, t):
                te.wait_ge(pt_lo, 6 * (i - 1) + 3 * t + 3)
                if t == 1:
                    te.wait_ge(ya_lo, 2 * (i - 1) + 1)
                for kb in range(NB):
                    n = T - P * kb
                    a = PT_AT[kb][2]
                    ins = mm3(ps[:, 7, P * kb:T], lambda part: vh[:, part, kb, P * t:P * t + P],
                              lambda part: pt[:, part, a:a + n], kb == 0, kb == NB - 1)
                ins.then_inc(pv_mm, 1)

            def att_step(i):
                scores(i, 0)
                gate_proj(i, 0)
                scores(i, 1)
                gate_proj(i, 1)
                prob_transposes(i, 0)
                te.wait_ge(siga_done, 2 * (i - 1) + 1)
                qk_proj(i, 0, 0)
                weighted(i, 0)
                prob_transposes(i, 1)
                te.wait_ge(siga_done, 2 * (i - 1) + 2)
                qk_proj(i, 0, 1)
                weighted(i, 1)
                te.wait_ge(att_lo, 6 * i + 1)
                qk_proj(i, 1, 0)
                te.wait_ge(att_lo, 6 * i + 2)
                qk_proj(i, 1, 1)
                v_proj(i)

            te.wait_ge(sigr_done, KD)
            qk_proj(0, 0, 0)
            te.wait_ge(mixa_done, KD)
            qk_proj(0, 0, 1)
            te.wait_ge(att_lo, 1)
            qk_proj(0, 1, 0)
            te.wait_ge(att_lo, 2)
            qk_proj(0, 1, 1)
            v_proj(0)
            with te.Fori(1, H // 2) as i:
                att_step(i)
            last = H // 2
            scores(last, 0)
            gate_proj(last, 0)
            scores(last, 1)
            gate_proj(last, 1)

            def pra_first(k0, k1, t):
                for k in range(k0, k1):
                    te.wait_ge(ya_lo, k + 1)
                    ins = mm3(ps[:, t, :], w_tile(C_PRA % 2, k, t, 256), features(yatt, k), k == 0, k == KD - 1)
                return ins
            te.wait_ge(w_lo, whole(C_PRA))
            prob_transposes(last, 0)
            te.wait_ge(siga_done, KD - 1)
            pra_first(0, H - 2, 0)
            weighted(last, 0)
            prob_transposes(last, 1)
            te.wait_ge(siga_done, KD)
            pra_first(0, H - 2, 1)
            weighted(last, 1)
            for t in range(2):
                pra_first(H - 2, H - 1, t)

            for t in range(2):
                pra_first(H - 1, H, t).then_inc(tile0 if t == 0 else w_used, 1)
            for cc in range(1, 4):
                te.wait_ge(w_lo, whole(C_PRA + cc))
                for t in range(2):
                    jt = 2 * cc + t
                    if cc == 1:
                        te.wait_ge(s_add, 4 * H)
                    else:
                        te.wait_ge(mb_mul, jt - 3)
                    project(C_PRA + cc, yatt, 2 * (cc % 2) + t, t).then_inc(tile0 if t == 0 else w_used, 1)

            def x1_transposes(half, blocks=range(NB)):
                for b in blocks:
                    for j in range(4):
                        ins = te.transpose(ps[:, 4 + b, P * j:P * j + P], x1T[:, 4 * half + j, P * b:P * b + P],
                                           ident[:, :])
                    ins.then_inc(x1n_mm, 1)
            for cc in range(4):
                te.wait_ge(w_lo, whole(C_OUT + cc))
                for t in range(2):
                    jt = 2 * cc + t
                    bank = 2 * (cc % 2) + t
                    if cc < 2:
                        te.wait_ge(mb_mul, 5 + jt)
                    else:
                        te.wait_ge(x1_done, jt - 3)
                    project(C_OUT + cc, h, bank, t, ready=(lambda k: te.wait_ge(mb_lo, k + 1)) if jt == 0 else None)\
                        .then_inc(tile0 if t == 0 else w_used, 1)
                    if jt == 4:
                        te.wait_ge(x1_done, 4)
                        x1_transposes(0)
            te.wait_ge(x1n_done, NB)
            te.wait_ge(x1_done, KD)
            x1_transposes(1, (0, 1))
            te.wait_ge(sq_added, KD)
            for b in range(NB):
                ins = te.matmul(ps[:, 2, b:b + 1], sqacc[:, P * b:P * b + P], ones[:, 0:1], start=True, stop=True)
            ins.then_inc(ms2_mm, 1)
            x1_transposes(1, (2,))
            keep_clock(8)
            te.wait_ge(diag_done, NB)
            te.matmul(ps[:, 3, :], ones[:, :], diag[:, :], start=True, stop=True).then_inc(rs2_mm, 1)
            x1_transposes(1, (3,))
            keep_clock(8)

            def up_step(i, peeled=False):
                te.wait_ge(w_lo, whole(C_UP, i))
                if peeled:
                    project2(C_UP, h, 0, lambda k: te.wait_ge(h2_lo, k + 1))
                else:
                    te.wait_ge(fconv_tap, 4 * i)
                    project(C_UP, h, 0, 0).then_inc(tile0, 1)
                    project(C_UP, h, 1, 1).then_inc(w_used, 1)
                te.wait_ge(w_lo, whole(C_UP + 1, i))
                wait_from(te, act_done, 2 * i)
                project(C_UP + 1, h, 2, 0).then_inc(tile0, 1)
                project(C_UP + 1, h, 3, 1).then_inc(w_used, 1)

            up_step(0, peeled=True)
            te.wait_ge(x1n_done, 2 * NB)
            with te.Fori(1, 7) as i:
                up_step(i)
                ada_total(9 + i)
            with te.Fori(7, NF // 2) as i:
                up_step(i)

            def down_half(s, u, b, half, start, stop):
                return mm3(ps[:, 2 * b + half, :], lambda part: act_s[:, 2 * s + u, part, P * b:P * b + P],
                           lambda part: wsplit[:, s, part, D * u + T * half:D * u + T * half + T], start, stop)

            def down_chunk(c0, i=0, start=False):
                te.wait_ge(w_lo, whole(c0, i))
                te.wait_ge(act_lo, 2 * (c0 - C_DOWN) + 2 + 4 * i)
                for u in range(2):
                    for b in (2, 3, 0, 1):
                        if start and u == 0 and b == 2:
                            te.wait_ge(ada_out, 16)
                        if start and u == 0 and b == 0:
                            te.wait_ge(act_done, NF)
                        for half in range(2):
                            ins = down_half(c0 % 2, u, b, half, start and u == 0, False)
                ins.then_inc(w_used, 1)

            down_chunk(C_DOWN, start=True)
            down_chunk(C_DOWN + 1)
            with te.Fori(1, NF // 4 - 1) as i:
                down_chunk(C_DOWN, i)
                down_chunk(C_DOWN + 1, i)
            te.wait_ge(w_lo, whole(C_END - 2))
            te.wait_ge(act_lo, NF - 2)
            for b in range(NB):
                for half in range(2):
                    down_half(0, 0, b, half, False, False)
            te.wait_ge(w_lo, whole(C_END - 1))
            te.wait_ge(act_lo, NF)
            for b in range(NB):
                for half in range(2):
                    down_half(0, 1, b, half, False, False)
                    down_half(1, 0, b, half, False, False)
                    down_half(1, 1, b, half, False, True).then_inc(down_mm, 1)


INPUTS = ["x", "c", "w_ada", "b_ada", "g_norm1", "w_in", "w_rnn_conv", "b_rnn_conv", "w_lru_a", "b_lru_a",
          "w_lru_i", "b_lru_i", "lru_lambda", "b_fgate", "w_proj_rnn", "w_proj_attn", "w_out", "g_norm2",
          "w_ffn_up", "w_ffn_conv", "b_ffn_conv", "w_ffn_down", "w_ada_final", "b_ada_final", "g_final"]


def kernel(**inputs):
    import numpy as np
    import concourse.bacc as bacc
    from concourse.bass_utils import run_bass_kernel_spmd

    nc = bacc.Bacc("TRN2", target_bir_lowering=False, num_devices=1)
    arrays, args = {}, []
    for name in INPUTS:
        a = np.ascontiguousarray(inputs[name])
        arrays[f"in_{name}"] = a
        args.append(nc.dram_tensor(f"in_{name}", a.shape, mybir.dt.from_np(a.dtype), kind="ExternalInput").ap())
    args.append(nc.dram_tensor("out_x", (1, T, D), FP32, kind="ExternalOutput").ap())
    hybrid_block(nc, *args)
    r = run_bass_kernel_spmd(nc, [arrays], core_ids=[0])
    return r.results[0]["out_x"]
```
